# Optimizing a Trainium2 kernel written in Bass

```python
import math
import jax, jax.numpy as jnp
from jax import lax
import numpy as np

D_MODEL = 1024
BATCH = 1
SEQ = 512
DEPTH = 2

N_EVEN = (DEPTH + 1) // 2
N_ODD = DEPTH // 2
RMS_EPS = 1e-6
D_FF = 2816
MAX_POS_OFFSET = 1024

GLA_HEADS = 4
GLA_DK = 128
GLA_DV = 256
GLA_QK = GLA_HEADS * GLA_DK
GLA_V = GLA_HEADS * GLA_DV
GLA_GATE_RANK = 16
GLA_GATE_NORMALIZER = 16.0
GLA_CHUNK = 64

SSM_HEADS = 16
SSM_HEADDIM = 64
SSM_DINNER = SSM_HEADS * SSM_HEADDIM
SSM_GROUPS = 4
SSM_DSTATE = 128
SSM_CONV = 4
SSM_CHUNK = 64
SSM_CONV_DIM = SSM_DINNER + 2 * SSM_GROUPS * SSM_DSTATE

AB_SPLITS = (GLA_QK, GLA_QK, GLA_V, GLA_V, GLA_GATE_RANK, SSM_DINNER, SSM_CONV_DIM, SSM_HEADS)
AB_IN = sum(AB_SPLITS)
AB_CAT = GLA_V + SSM_DINNER

MLA_HEADS = 8
MLA_Q_RANK = 384
MLA_KV_RANK = 256
MLA_NOPE = 128
MLA_ROPE = 64
MLA_V = 128
MLA_QK = MLA_NOPE + MLA_ROPE
MLA_DOWN = MLA_Q_RANK + MLA_KV_RANK + MLA_ROPE
ROPE_THETA = 10000.0
ATTN_BLOCK = 128

kernel_name = "hybrid_gla_ssd_mla_macaron"

def rmsnorm(x, w):
    xf = x.astype(jnp.float32)
    y = xf * lax.rsqrt(jnp.mean(xf * xf, axis=-1, keepdims=True) + RMS_EPS)
    return (y * w.astype(jnp.float32)).astype(x.dtype)

def swiglu(h, w_gate, w_up, w_down):
    return (jax.nn.silu(h @ w_gate) * (h @ w_up)) @ w_down

def gla_chunked(q, k, v, log_a):
    b_, t, h, dk = q.shape
    dv = v.shape[-1]
    nc = t // GLA_CHUNK
    f32 = jnp.float32

    def chunks(u):
        return u.astype(f32).reshape(b_, nc, GLA_CHUNK, h, u.shape[-1]).transpose(1, 0, 3, 2, 4)

    qc, kc, vc = chunks(q), chunks(k), chunks(v)
    bc = jnp.cumsum(chunks(log_a), axis=-2)
    causal = jnp.tril(jnp.ones((GLA_CHUNK, GLA_CHUNK), dtype=bool))[:, :, None]

    def step(state, inp):
        qi, ki, vi, bi = inp
        b_last = bi[:, :, -1:, :]
        o_inter = jnp.einsum('bhik,bhkv->bhiv', qi * jnp.exp(bi), state)
        decay = jnp.exp(jnp.where(causal, bi[:, :, :, None, :] - bi[:, :, None, :, :], -jnp.inf))
        scores = jnp.einsum('bhik,bhijk->bhij', qi, decay * ki[:, :, None, :, :])
        o = o_inter + jnp.einsum('bhij,bhjv->bhiv', scores, vi)
        k_dec = ki * jnp.exp(b_last - bi)
        state = state * jnp.exp(b_last)[:, :, 0, :, None] + jnp.einsum('bhjk,bhjv->bhkv', k_dec, vi)
        return state, o

    s0 = jnp.zeros((b_, h, dk, dv), f32)
    _, out = lax.scan(step, s0, (qc, kc, vc, bc))
    return out.transpose(1, 0, 3, 2, 4).reshape(b_, t, h, dv).astype(v.dtype)

def segsum(a):
    n = a.shape[-1]
    cs = jnp.cumsum(a, axis=-1)
    mask = jnp.tril(jnp.ones((n, n), dtype=bool))
    return jnp.where(mask, cs[..., :, None] - cs[..., None, :], -jnp.inf)

def ssd_chunked(x, a, bm, cm):
    b_, t, h, p = x.shape
    g, n = bm.shape[-2:]
    r = h // g
    c = t // SSM_CHUNK
    l = SSM_CHUNK
    x = x.reshape(b_, c, l, g, r, p)
    a = a.reshape(b_, c, l, g, r).transpose(0, 3, 4, 1, 2)
    bm = bm.reshape(b_, c, l, g, n)
    cm = cm.reshape(b_, c, l, g, n)
    a_cum = jnp.cumsum(a, axis=-1)
    decay_in = jnp.exp(segsum(a))
    cb = jnp.einsum('bclgn,bcsgn->bgcls', cm, bm)
    y_diag = jnp.einsum('bgrcls,bcsgrp->bclgrp', cb[:, :, None] * decay_in, x)
    decay_states = jnp.exp(a_cum[..., -1:] - a_cum).transpose(0, 3, 4, 1, 2)
    states = jnp.einsum('bcsgn,bcsgrp->bcgrpn', bm, x * decay_states[..., None])
    states = jnp.concatenate([jnp.zeros_like(states[:, :1]), states], axis=1)
    chunk_decay = jnp.exp(segsum(jnp.pad(a_cum[..., -1], ((0, 0), (0, 0), (0, 0), (1, 0)))))
    states = jnp.einsum('bgrzc,bcgrpn->bzgrpn', chunk_decay, states)[:, :-1]
    y_off = jnp.einsum('bclgn,bcgrpn->bclgrp', cm, states) * jnp.exp(a_cum).transpose(0, 3, 4, 1, 2)[..., None]
    return (y_diag + y_off).reshape(b_, t, h, p)

def causal_depthwise_conv(u, w, bias):
    ch = u.shape[-1]
    out = lax.conv_general_dilated(u, w[:, None, :].astype(u.dtype), window_strides=(1,),
                                   padding=[(SSM_CONV - 1, 0)], dimension_numbers=('NWC', 'WIO', 'NWC'),
                                   feature_group_count=ch)
    return out + bias.astype(u.dtype)

def gla_ssd_mixer(h, w_in, gla_w_gate2, gla_b_gate2, gla_norm_w, conv_w, conv_b, dt_bias, a_log,
                  d_skip, ssm_norm_w, w_out):
    f32 = jnp.float32
    b_, t, _ = h.shape
    points, acc = [], 0
    for s in AB_SPLITS[:-1]:
        acc += s
        points.append(acc)
    q, k, v, g, a_low, z, xbc, dt = jnp.split(h @ w_in, points, axis=-1)
    q = q.reshape(b_, t, GLA_HEADS, GLA_DK) * (GLA_DK ** -0.5)
    k = k.reshape(b_, t, GLA_HEADS, GLA_DK)
    v = v.reshape(b_, t, GLA_HEADS, GLA_DV)
    log_a = jax.nn.log_sigmoid((a_low @ gla_w_gate2 + gla_b_gate2).astype(f32)) / GLA_GATE_NORMALIZER
    o = gla_chunked(q, k, v, log_a.reshape(b_, t, GLA_HEADS, GLA_DK))
    o = rmsnorm(o, gla_norm_w) * jax.nn.silu(g.reshape(b_, t, GLA_HEADS, GLA_DV))
    o_gla = o.reshape(b_, t, GLA_V)
    xbc = jax.nn.silu(causal_depthwise_conv(xbc, conv_w, conv_b))
    xs, bm, cm = jnp.split(xbc, [SSM_DINNER, SSM_DINNER + SSM_GROUPS * SSM_DSTATE], axis=-1)
    dt = jax.nn.softplus(dt.astype(f32) + dt_bias.astype(f32))
    a = -jnp.exp(a_log.astype(f32))
    xs = xs.reshape(b_, t, SSM_HEADS, SSM_HEADDIM).astype(f32)
    y = ssd_chunked(xs * dt[..., None], dt * a,
                    bm.reshape(b_, t, SSM_GROUPS, SSM_DSTATE).astype(f32),
                    cm.reshape(b_, t, SSM_GROUPS, SSM_DSTATE).astype(f32))
    y = y + d_skip.astype(f32)[:, None] * xs
    y = y.reshape(b_, t, SSM_DINNER) * jax.nn.silu(z.astype(f32))
    gs = SSM_DINNER // SSM_GROUPS
    y = rmsnorm(y.reshape(b_, t, SSM_GROUPS, gs), ssm_norm_w.reshape(SSM_GROUPS, gs))
    y = y.reshape(b_, t, SSM_DINNER).astype(h.dtype)
    return jnp.concatenate([o_gla, y], axis=-1) @ w_out

def apply_rope(u, cos, sin):
    u1, u2 = jnp.split(u, 2, axis=-1)
    return jnp.concatenate([u1 * cos - u2 * sin, u2 * cos + u1 * sin], axis=-1).astype(u.dtype)

def mla_mixer(h, positions, w_down, q_norm_w, w_uq, kv_norm_w, w_ukv, w_o):
    f32 = jnp.float32
    b_, t, _ = h.shape
    cq, ckv, k_rope = jnp.split(h @ w_down, [MLA_Q_RANK, MLA_Q_RANK + MLA_KV_RANK], axis=-1)
    q = (rmsnorm(cq, q_norm_w) @ w_uq).reshape(b_, t, MLA_HEADS, MLA_QK)
    q_nope, q_rope = q[..., :MLA_NOPE], q[..., MLA_NOPE:]
    kv = (rmsnorm(ckv, kv_norm_w) @ w_ukv).reshape(b_, t, MLA_HEADS, MLA_NOPE + MLA_V)
    k_nope, v = kv[..., :MLA_NOPE], kv[..., MLA_NOPE:]
    inv_freq = ROPE_THETA ** (-jnp.arange(0, MLA_ROPE, 2, dtype=f32) / MLA_ROPE)
    ang = positions.astype(f32)[..., None] * inv_freq
    cos, sin = jnp.cos(ang), jnp.sin(ang)
    q_rope = apply_rope(q_rope, cos[:, :, None, :], sin[:, :, None, :])
    k_rope = apply_rope(k_rope, cos, sin)
    scale = MLA_QK ** -0.5
    outs = []
    for start in range(0, t, ATTN_BLOCK):
        end = start + ATTN_BLOCK
        s = (jnp.einsum('bqhd,bkhd->bhqk', q_nope[:, start:end], k_nope[:, :end])
             + jnp.einsum('bqhd,bkd->bhqk', q_rope[:, start:end], k_rope[:, :end])).astype(f32) * scale
        mask = (start + jnp.arange(ATTN_BLOCK))[:, None] >= jnp.arange(end)[None, :]
        p = jax.nn.softmax(jnp.where(mask, s, -jnp.inf), axis=-1).astype(v.dtype)
        outs.append(jnp.einsum('bhqk,bkhd->bqhd', p, v[:, :end]))
    o = jnp.concatenate(outs, axis=1).reshape(b_, t, MLA_HEADS * MLA_V)
    return o @ w_o

def setup_inputs(seed: int = 0) -> dict:
    key = jax.random.key(seed)
    keys = list(jax.random.split(key, 64))
    f32 = jnp.float32

    def nk():
        return keys.pop()

    def w(shape, fan_in):
        return jax.random.normal(nk(), shape, f32) * (fan_in ** -0.5)

    def gain(shape):
        return 1.0 + 0.05 * jax.random.normal(nk(), shape, f32)

    def bias(shape, s=0.02):
        return s * jax.random.normal(nk(), shape, f32)

    d, fdim = D_MODEL, D_FF
    x = jax.random.normal(nk(), (BATCH, SEQ, D_MODEL), f32)
    positions = (jax.random.randint(nk(), (BATCH, 1), 0, MAX_POS_OFFSET, dtype=jnp.int32)
                 + jnp.arange(SEQ, dtype=jnp.int32)[None, :])
    dt0 = jnp.exp(jax.random.uniform(nk(), (N_EVEN, SSM_HEADS), f32, math.log(1e-3), math.log(1e-1)))
    dt_bias = dt0 + jnp.log(-jnp.expm1(-dt0))
    a_log = jnp.log(jax.random.uniform(nk(), (N_EVEN, SSM_HEADS), f32, 1.0, 16.0))
    return {
        "x": x,
        "positions": positions,
        "ffn1_pre_norm": gain((DEPTH, d)),
        "ffn1_w_gate": w((DEPTH, d, fdim), d),
        "ffn1_w_up": w((DEPTH, d, fdim), d),
        "ffn1_w_down": w((DEPTH, fdim, d), fdim),
        "ffn1_post_norm": gain((DEPTH, d)),
        "mix_pre_norm": gain((DEPTH, d)),
        "mix_post_norm": gain((DEPTH, d)),
        "ffn2_pre_norm": gain((DEPTH, d)),
        "ffn2_w_gate": w((DEPTH, d, fdim), d),
        "ffn2_w_up": w((DEPTH, d, fdim), d),
        "ffn2_w_down": w((DEPTH, fdim, d), fdim),
        "ffn2_post_norm": gain((DEPTH, d)),
        "ab_w_in": w((N_EVEN, d, AB_IN), d),
        "gla_w_gate2": w((N_EVEN, GLA_GATE_RANK, GLA_QK), GLA_GATE_RANK),
        "gla_b_gate2": bias((N_EVEN, GLA_QK), 0.1),
        "gla_norm": gain((N_EVEN, GLA_DV)),
        "ssm_conv_w": w((N_EVEN, SSM_CONV, SSM_CONV_DIM), SSM_CONV),
        "ssm_conv_b": bias((N_EVEN, SSM_CONV_DIM)),
        "ssm_dt_bias": dt_bias,
        "ssm_a_log": a_log,
        "ssm_d": 1.0 + 0.1 * jax.random.normal(nk(), (N_EVEN, SSM_HEADS), f32),
        "ssm_norm": gain((N_EVEN, SSM_DINNER)),
        "ab_w_out": w((N_EVEN, AB_CAT, d), AB_CAT),
        "mla_w_down": w((N_ODD, d, MLA_DOWN), d),
        "mla_q_norm": gain((N_ODD, MLA_Q_RANK)),
        "mla_w_uq": w((N_ODD, MLA_Q_RANK, MLA_HEADS * MLA_QK), MLA_Q_RANK),
        "mla_kv_norm": gain((N_ODD, MLA_KV_RANK)),
        "mla_w_ukv": w((N_ODD, MLA_KV_RANK, MLA_HEADS * (MLA_NOPE + MLA_V)), MLA_KV_RANK),
        "mla_w_o": w((N_ODD, MLA_HEADS * MLA_V, d), MLA_HEADS * MLA_V),
    }

def reference(x, positions, ffn1_pre_norm, ffn1_w_gate, ffn1_w_up, ffn1_w_down, ffn1_post_norm,
              mix_pre_norm, mix_post_norm, ffn2_pre_norm, ffn2_w_gate, ffn2_w_up, ffn2_w_down,
              ffn2_post_norm, ab_w_in, gla_w_gate2, gla_b_gate2, gla_norm, ssm_conv_w, ssm_conv_b,
              ssm_dt_bias, ssm_a_log, ssm_d, ssm_norm, ab_w_out, mla_w_down, mla_q_norm, mla_w_uq,
              mla_kv_norm, mla_w_ukv, mla_w_o):
    for i in range(DEPTH):
        f = swiglu(rmsnorm(x, ffn1_pre_norm[i]), ffn1_w_gate[i], ffn1_w_up[i], ffn1_w_down[i])
        x = x + 0.5 * rmsnorm(f, ffn1_post_norm[i])
        h = rmsnorm(x, mix_pre_norm[i])
        j = i // 2
        if i % 2 == 0:
            m = gla_ssd_mixer(h, ab_w_in[j], gla_w_gate2[j], gla_b_gate2[j], gla_norm[j], ssm_conv_w[j],
                              ssm_conv_b[j], ssm_dt_bias[j], ssm_a_log[j], ssm_d[j], ssm_norm[j], ab_w_out[j])
        else:
            m = mla_mixer(h, positions, mla_w_down[j], mla_q_norm[j], mla_w_uq[j], mla_kv_norm[j],
                          mla_w_ukv[j], mla_w_o[j])
        x = x + rmsnorm(m, mix_post_norm[i])
        f = swiglu(rmsnorm(x, ffn2_pre_norm[i]), ffn2_w_gate[i], ffn2_w_up[i], ffn2_w_down[i])
        x = x + 0.5 * rmsnorm(f, ffn2_post_norm[i])
    return x


_drawn_inputs = setup_inputs


def setup_inputs(seed=0):
    import zlib

    import numpy as np

    out = dict(_drawn_inputs(seed))
    spreads = {}
    factors = {'gla_b_gate2': 3.225, 'gla_norm': 2.99, 'mla_q_norm': 2.867, 'ssm_conv_b': 3.346}
    for name, (base, spread) in spreads.items():
        noise = np.random.default_rng([zlib.crc32(name.encode()), seed]).standard_normal(out[name].shape)
        drawn = base * np.exp(spread * noise) if base else spread * noise
        out[name] = __import__('jax').numpy.asarray(drawn.astype(out[name].dtype))
    for name, factor in factors.items():
        out[name] = (out[name] * factor).astype(out[name].dtype)
    return out
```

```python
from contextlib import ExitStack, contextmanager

import numpy as np

import concourse.bass as bass
from concourse import mybir

F32 = mybir.dt.float32
F32R = mybir.dt.float32r
I32 = mybir.dt.int32
U8 = mybir.dt.uint8
ALU = mybir.AluOpType
ACT = mybir.ActivationFunctionType
AX_X = mybir.AxisListType.X
ds = bass.ds

P = 128
T = 512
NC = T // P
D = 1024
DK = D // P
F = 2816
FT = F // P
EPS = 1e-6
N_FFN = 4
N_SUB = 6
EVEN, ODD = 1, 4

GH, GDV = 4, 256
RANK = 16
SPANS = (64, 32, 16, 8, 4, 2, 1)
SH, SP_, SG = 16, 64, 4
DT0 = 32
MH, QR, KR, ROPE = 8, 3, 2, 64

RAW = 2
RING = 4
HALF = FT // 2
WIDTH = HALF * P
FFN_OF = {0: 0, 2: 1, 3: 2, 5: 3}
SCORE_SCALE = (P + ROPE) ** -0.5

ROUND = 1.5 * 2 ** 23
TURN_1 = 6.28125
TURN_2 = float(np.float32(round((2 * np.pi - TURN_1) * 2 ** 20) / 2 ** 20))
TURN = (TURN_1, TURN_2, 2 * np.pi - TURN_1 - TURN_2)
PI_BELOW = float(np.nextafter(np.float32(np.pi), np.float32(0)))


def plan_stages():
    ffn = [[(f"gate_up{f}", 2 * FT, DK * P), (f"down{f}", 2 * DK, WIDTH)] for f in range(N_FFN)]
    even = [("qk_small", 2 * GH + 1, D), ("v", 8, D), ("g", 8, D), ("z", 8, D), ("xbc", 16, D), ("even_out", 16, D)]
    odd = [("latent", 6, D), ("q_up", 4, 9 * P), ("k_up", 2, D), ("v_up", 2, D), ("odd_out", 8, D)]
    stages, first = {}, 0
    for name, slots, width in ffn[0] + even + ffn[1] + ffn[2] + odd + ffn[3]:
        stages[name] = (first, slots, width)
        first += slots
    return stages, first


def plan_norms():
    names = []
    for s in range(N_SUB):
        names.append((s, "pre"))
        if s == EVEN:
            names += [("gla", h) for h in range(GH)] + [("ssm", g) for g in range(SG)]
        if s == ODD:
            names += ["q_latent", "kv_latent"]
        names.append((s, "post"))
    return {name: n for n, name in enumerate(names)}


def build_trunk(nc, dram, out):
    stages, total_slots = plan_stages()
    norms = plan_norms()

    def width_of(slot):
        for first, slots, width in stages.values():
            if first <= slot < first + slots:
                return width

    with ExitStack() as ctx:
        def sb(name, shape, dt=F32):
            return ctx.enter_context(nc.sbuf_tensor(name, shape, dt))

        def sem(name):
            return ctx.enter_context(nc.semaphore(name))

        x = sb("x", [P, DK, T])
        raw = [sb(f"raw{r}", [P, WIDTH]) for r in range(RAW)]
        w_hi = [sb(f"w_hi{r}", [P, WIDTH], F32R) for r in range(RING)]
        w_lo = [sb(f"w_lo{r}", [P, WIDTH], F32R) for r in range(RING)]
        scaled = [sb(f"scaled{b}", [P, T]) for b in range(2)]
        other = [sb(f"other{b}", [P, T]) for b in range(2)]
        square = other
        diag = other[1][:, :].rearrange("p (c t) -> p c t", c=NC)
        rstd = sb("rstd", [P, T])
        square_sum = sb("square_sum", [P, T])
        ident = sb("ident", [P, P])
        ones = sb("ones", [P, P])
        gains = sb("gains", [P, 2 * N_SUB * DK])
        mixer_cols = sb("mixer_cols", [P, 132])
        mean = sb("mean", [P, NC])
        rstd_col = sb("rstd_col", [P, NC])
        minus_half = sb("minus_half", [P, NC])

        def pre_gain(s):
            return gains[:, DK * s:DK * s + DK]

        def post_gain(s):
            return gains[:, DK * (N_SUB + s):DK * (N_SUB + s) + DK]

        conv_w = mixer_cols[:, 0:64].rearrange("p (i k) -> p i k", k=4)
        conv_b = mixer_cols[:, 64:80]
        gla_bias = mixer_cols[:, 80:84]
        gla_gain = mixer_cols[:, 84:86]
        skip_col = mixer_cols[:, 86:94]
        ssm_gain = mixer_cols[:, 94:102]
        dt_bias = mixer_cols[DT0:DT0 + SH, 102:103]
        a_log = mixer_cols[DT0:DT0 + SH, 103:104]
        latent_gain = mixer_cols[:, 104:109]
        inv_freq = mixer_cols[:, 109:110]


        HROWS, AROWS = 2 * DK, 2 * FT

        def parts(*shapes):
            with ExitStack() as inner:
                return [inner.enter_context(nc.sbuf_tensor(name, [P, rows, T], dt)) for name, rows, dt in shapes]

        o_hi, o_lo = parts(("o_hi", MH, F32R), ("o_lo", MH, F32R))
        cat_lo, = parts(("cat_lo", 16, F32R))
        h_rows, = parts(("h_rows", HROWS, F32))
        h_hi = sb("h_hi", [P, DK, T], F32R)
        h_lo = sb("h_lo", [P, DK, T], F32R)

        _, cat_hi = parts(("before_cat_hi", 16, F32), ("cat_hi", 16, F32R))
        _, latent_hi, latent_lo = parts(("before_latent", 32, F32), ("latent_hi", 5, F32R), ("latent_lo", 5, F32R))
        a_rows, = parts(("a_rows", AROWS, F32))
        a_hi = sb("a_hi", [P, FT, T], F32R)
        a_lo = sb("a_lo", [P, FT, T], F32R)

        def rows(region, at, count=1):
            if isinstance(at, int):
                return region[:, at:at + count, :].rearrange("p r t -> p (r t)")
            return region[:, :, :].rearrange("p r t -> p (r t)")[:, ds(at * T, count * T)]

        def rows_r(tensor, at):
            return rows(tensor, at)

        CAT, Q, K, V, XS, B_ROWS, C_ROWS = 0, 16, 20, 24, 16, 24, 28
        scores = rows(a_rows, 8, 4).rearrange("p (j i t) -> p j i t", j=NC, i=NC)
        v_head = rows(a_rows, 12, 2).rearrange("p (c v) -> p c v", c=NC)
        k_dec = [rows(a_rows, 14 + b) for b in range(2)]
        small = rows(a_rows, 32)
        gated = rows(a_rows, 33)
        head_rstd = rows(a_rows, 43)
        level_mask = rows(a_rows, 34)[:, 0:256].bitcast(U8).rearrange("p (l t) -> p l t", l=8)
        tri = rows(a_rows, 34)[:, 256:384]
        gate2 = rows(a_rows, 35)[0:RANK, :]
        ssm_cols = rows(a_rows, 36)[:, 0:14 * SH].rearrange("p (n h) -> p n h", h=SH)
        LOG_A = 37
        pad = [rows(a_rows, 37, 2)[:, 0:T + 3], rows(a_rows, 39, 2)[:, 0:T + 3]]
        dt_rows, cum, far1, far2 = [rows(a_rows, 37 + n)[DT0:DT0 + SH, :] for n in range(4)]
        head_row = [rows(a_rows, 41 + b)[DT0:DT0 + SH, :] for b in range(2)]
        x_group = rows(h_rows, 0, 2).rearrange("p (c v) -> p c v", c=NC)
        x_far = rows(h_rows, 2, 3).rearrange("p (n v) -> p n v", n=6)
        cb = rows(h_rows, 5, 4).rearrange("p (j i t) -> p j i t", j=NC, i=NC)
        decay = [rows(h_rows, 9 + b) for b in range(2)]
        from_start = [rows(h_rows, 11 + b) for b in range(2)]
        b_group = rows(h_rows, 13)
        xs_group = rows(h_rows, 14, 2).rearrange("p (m t) -> p m t", m=2)

        QN, QROPE, KN, VT, LATENT = 0, 8, 12, 20, 20
        cos, sin, krope = rows(a_rows, 28), rows(a_rows, 29), rows(a_rows, 30)
        causal, turn_mat = rows(a_rows, 31)[:, 0:P], rows(a_rows, 31)[:, P:2 * P]
        probs = rows(a_rows, 32, 4).rearrange("p (i k) -> p i k", i=NC)
        probs_t = rows(a_rows, 36, 4).rearrange("p (j q) -> p j q", j=NC)
        q_head, q_pair = rows(a_rows, 40), rows(a_rows, 41)
        v_pair = rows(a_rows, 42, 2).rearrange("p (c v) -> p c v", c=NC)
        angle = [rows(a_rows, row) for row in (42, 43, 30)]
        peak = mixer_cols[:, 112:116]
        peak_bias = mixer_cols[:, 116:120]
        prob_sum = mixer_cols[:, 120:124]
        chunk_decay = mixer_cols[:, 124:128]
        ssm_chunk_decay = mixer_cols[DT0:DT0 + SH, 128:132]

        def u_row(s, k):
            return rows(a_rows, {EVEN: CAT, ODD: VT}[s] + k) if s in (EVEN, ODD) else rows(h_rows, k)

        ps = ctx.enter_context(nc.psum_tensor("ps", [P, 8, T], F32))
        SUMS, SPREAD = 6, 7
        QK0, V0, G0, Z0, XBC0, LATENT0 = 0, 9, 17, 25, 33, 49

        consts_in, x_in, even_in, odd_in = sem("consts_in"), sem("x_in"), sem("even_in"), sem("odd_in")
        consts_made, gains_halved = sem("consts_made"), sem("gains_halved")
        raw_in = [sem(f"raw_in{r}") for r in range(RAW)]
        hi_done, lo_done = sem("hi_done"), sem("lo_done")
        slot_done = sem("slot_done")
        residual_ready, h_hi_ready, h_lo_ready = sem("residual_ready"), sem("h_hi_ready"), sem("h_lo_ready")
        pre_square, pre_summed = sem("pre_square"), sem("pre_summed")
        post_square, post_summed, u_ready = sem("post_square"), sem("post_summed"), sem("u_ready")
        sums_ready, mean_ready, rstd_col_ready = sem("sums_ready"), sem("mean_ready"), sem("rstd_col_ready")
        diag_ready, spread_ready, rstd_ready = sem("diag_ready"), sem("spread_ready"), sem("rstd_ready")
        gate_scaled, up_scaled, silu_done = sem("gate_scaled"), sem("up_scaled"), sem("silu_done")
        a_ready, a_hi_ready, a_lo_ready = sem("a_ready"), sem("a_hi_ready"), sem("a_lo_ready")
        dve_step, act_step, stored = sem("dve_step"), sem("act_step"), sem("stored")
        tile_taken, row_silu, conv_done = sem("tile_taken"), sem("row_silu"), sem("conv_done")
        decay_logits, logit_ready, softplus_ready = sem("decay_logits"), sem("logit_ready"), sem("softplus_ready")
        log_a_ready = sem("log_a_ready")
        gla_diff, gla_decay, gla_factors = sem("gla_diff"), sem("gla_decay"), sem("gla_factors")
        gla_products, gla_merged, far_taken = sem("gla_products"), sem("gla_merged"), sem("far_taken")
        key_copied, value_copied, gla_out = sem("key_copied"), sem("value_copied"), sem("gla_out")
        head_squares, head_summed, head_gated = sem("head_squares"), sem("head_summed"), sem("head_gated")
        dt_signal, dt_act, dt_cum, dt_far = sem("dt_signal"), sem("dt_act"), sem("dt_cum"), sem("dt_far")
        cols_turned, cols_ready = sem("cols_turned"), sem("cols_ready")
        group_copied, x_turned, x_taken, x_far_ready = sem("group_copied"), sem("x_turned"), sem("x_taken"), sem("x_far_ready")
        cb_ready, cb_taken, cb_far_taken = sem("cb_ready"), sem("cb_taken"), sem("cb_far_taken")
        head_row_ready, row_spread, from_start_ready = sem("head_row_ready"), sem("row_spread"), sem("from_start_ready")
        decay_diff, decay_exp, decay_ready = sem("decay_diff"), sem("decay_exp"), sem("decay_ready")
        y_diag_done, y_far_done, y_gated = sem("y_diag_done"), sem("y_far_done"), sem("y_gated")
        group_squares, group_summed, group_done = sem("group_squares"), sem("group_summed"), sem("group_done")
        cat_hi_ready, cat_lo_ready = sem("cat_hi_ready"), sem("cat_lo_ready")
        angle_ready, table_ready = sem("angle_ready"), sem("table_ready")
        latent_square, latent_summed, latent_normed = sem("latent_square"), sem("latent_summed"), sem("latent_normed")
        latent_hi_ready, latent_lo_ready = sem("latent_hi_ready"), sem("latent_lo_ready")
        q_taken, k_taken, v_taken = sem("q_taken"), sem("k_taken"), sem("v_taken")
        rope_turned, rope_taken, rope_done = sem("rope_turned"), sem("rope_taken"), sem("rope_done")
        pair_copied, q_copied, scores_done, bias_ready = sem("pair_copied"), sem("q_copied"), sem("scores_done"), sem("bias_ready")
        exp_done, probs_ready, probs_turned = sem("exp_done"), sem("probs_ready"), sem("probs_turned")
        turned_dve, turned_act, att_done = sem("turned_dve"), sem("turned_act"), sem("att_done")
        o_hi_ready, o_lo_ready = sem("o_hi_ready"), sem("o_lo_ready")

        block = ctx.enter_context(nc.Block())

        def end_of(name):
            return stages[name][0] + stages[name][1]

        def diagonal(blocks):
            first = blocks[:, :, 0, :]
            (part, row, col) = first.ap
            return bass.AP(tensor=first.tensor, offset=first.offset, ap=[list(part), [row[0] + P, NC], list(col)])

        FAR = [(0, 1), (1, 2), (2, 3), (0, 2), (1, 3), (0, 3)]

        @block.sync
        def _(sp):
            sp.dma_start(ident[:, :], dram["ident"]).then_inc(consts_in, 16)
            sp.dma_start(gains[:, :], dram["gains"]).then_inc(consts_in, 16)
            sp.dma_start(mixer_cols[:, 0:110], dram["mixer_cols"]).then_inc(consts_in, 16)
            sp.dma_start(x[:, :, :], dram["x_t"].rearrange("(k p) t -> p k t", p=P)).then_inc(x_in, 16)

            def load_slot(src, index, slot, turns, width):
                if slot >= RAW or not isinstance(turns, int):
                    sp.wait_ge(lo_done, slot - 1 + turns)
                sp.dma_start(raw[slot % RAW][:, 0:width], src[index]).then_inc(raw_in[slot % RAW], 16)

            for name, (first, slots, width) in stages.items():
                src = dram["w_" + name]
                turns = slots // 4
                if turns > 1 and first >= RAW:
                    with sp.Fori(0, turns) as turn:
                        for n in range(4):
                            load_slot(src, turn * 4 + n, first + n, turn * 4, width)
                    for n in range(4 * turns, slots):
                        load_slot(src, n, first + n, 0, width)
                    continue
                for n in range(min(slots, 4)):
                    load_slot(src, n, first + n, 0, width)
                if turns > 1:
                    with sp.Fori(1, turns) as turn:
                        for n in range(4):
                            load_slot(src, turn * 4 + n, first + n, turn * 4, width)
                for n in range(max(4, 4 * turns), slots):
                    load_slot(src, n, first + n, 0, width)
            sp.wait_ge(residual_ready, DK * N_SUB)
            sp.dma_start(out.rearrange("(k p) t -> p k t", p=P), x[:, :, :]).then_inc(stored, 16)
            sp.wait_ge(stored, 16)

        @block.gpsimd
        def _(pool):
            nc.gpsimd.memset(ones[:, :], 1.0).then_inc(consts_made, 1)
            nc.gpsimd.memset(minus_half[:, :], -0.5).then_inc(consts_made, 1)
            pool.wait_ge(consts_made, 2)

            def split_low(slot, turns, width):
                pool.wait_ge(hi_done, slot + 1 + turns)
                if slot >= RING:
                    pool.wait_ge(slot_done, slot - RING + 1 + turns)
                nc.gpsimd.tensor_tensor(w_lo[slot % RING][:, 0:width], raw[slot % RAW][:, 0:width],
                                        w_hi[slot % RING][:, 0:width].bitcast(F32), ALU.subtract).then_inc(lo_done, 1)

            def split_stage(name, done=0):
                first, slots, width = stages[name]
                turns = (slots - done) // 4
                if turns:
                    with pool.Fori(0, turns) as turn:
                        for n in range(4):
                            split_low(first + done + n, turn * 4, width)
                for n in range(done + 4 * turns, slots):
                    split_low(first + n, 0, width)

            def split_some(name, start, stop):
                first = stages[name][0]
                for n in range(start, stop):
                    split_low(first + n, 0, width_of(first + n))

            def power(n):
                pool.wait_ge(mean_ready, n + 1)
                nc.gpsimd.tensor_tensor(rstd_col[:, :], mean[:, :], minus_half[:, :], ALU.pow).then_inc(rstd_col_ready, 1)

            def pre_sum(s):
                for k in range(1, DK):
                    pool.wait_ge(pre_square, DK * s + k + 1)
                    if k > 1:
                        pool.wait_ge(pre_summed, (DK - 1) * s + k - 1)
                    nc.gpsimd.tensor_tensor(square_sum[:, :], square_sum[:, :], square[k % 2][:, :], ALU.add).then_inc(pre_summed, 1)
                power(norms[(s, "pre")])

            first_stage = ["gate_up0", "qk_small", "gate_up1", "gate_up2", "latent", "gate_up3"]
            last_stage = ["down0", "even_out", "down1", "down2", "odd_out", "down3"]
            split_some("gate_up0", 0, 2)
            for s in range(N_SUB):
                split_some(first_stage[s], 2, RING)
                pre_sum(s)
                split_stage(first_stage[s], RING)
                if s == EVEN:
                    split_stage("v")
                    split_stage("g")
                    split_some("z", 0, RING)
                    with pool.Fori(0, GH) as h:
                        power(h + norms[("gla", 0)])
                    split_some("z", RING, 8)
                    split_stage("xbc")
                    split_some("even_out", 0, RING)
                    with pool.Fori(0, SG) as g:
                        power(g + norms[("ssm", 0)])
                    split_stage("even_out", RING)
                elif s == ODD:
                    split_stage("q_up")
                    power(norms["q_latent"])
                    power(norms["kv_latent"])
                    split_stage("k_up")
                    split_stage("v_up")
                    split_stage("odd_out")
                else:
                    split_stage(last_stage[s])
                if s + 1 < N_SUB:
                    split_some(first_stage[s + 1], 0, 2)
                power(norms[(s, "post")])

        @block.scalar
        def _(act):
            steps = [0]

            def after(ins, turns=0, per_turn=0):
                steps[0] += 1
                ins.then_inc(act_step, 1)
                act.wait_ge(act_step, turns * per_turn + steps[0] if per_turn else steps[0])

            def copy(to, source, scale=1.0):
                return nc.scalar.activation(to, source, ACT.Copy, scale=scale)

            def split_high(slot, turns, width):
                act.wait_ge(raw_in[slot % RAW], 16 * (slot // RAW + 1) + turns * 8)
                if slot >= RING:
                    act.wait_ge(slot_done, slot - RING + 1 + turns)
                    act.wait_ge(lo_done, slot - RING + 1 + turns)
                copy(w_hi[slot % RING][:, 0:width], raw[slot % RAW][:, 0:width]).then_inc(hi_done, 1)

            def split_then(name, per_tile, take):
                first, slots, width = stages[name]
                per_turn, tiles = 4 // per_tile, slots // per_tile
                turns = max(0, slots - RING) // 4
                if turns > 1:
                    with act.Fori(0, turns) as turn:
                        for n in range(per_turn):
                            for m in range(per_tile):
                                split_high(first + RING + n * per_tile + m, turn * 4, width)
                            take(turn * per_turn + n, n)
                else:
                    turns = 0
                for tile in range(turns * per_turn, tiles):
                    last = tile == tiles - 1
                    if last:
                        take(tile, tile % per_turn)
                    for m in range(per_tile):
                        slot = first + RING + tile * per_tile + m
                        if slot < total_slots:
                            split_high(slot, 0, width_of(slot))
                    if not last:
                        take(tile, tile % per_turn)

            def pre_norm(s):
                for k in range(DK):
                    if s:
                        act.wait_ge(residual_ready, DK * (s - 1) + k + 1)
                    copy(h_hi[:, k, :], x[:, k, :], pre_gain(s)[:, k:k + 1]).then_inc(h_hi_ready, 1)
                    if k >= 3:
                        act.wait_ge(pre_summed, (DK - 1) * s + k - 2)
                    nc.scalar.activation(square_sum[:, :] if k == 0 else square[k % 2][:, :], x[:, k, :],
                                         ACT.Square).then_inc(pre_square, 1)

            def take_out(s, name, per_tile):
                region, base = {EVEN: (a_rows, CAT), ODD: (a_rows, VT)}.get(s, (h_rows, 0))

                def take(tile, n):
                    b = n % 2
                    act.wait_ge(slot_done, tile * per_tile + (stages[name][0] + per_tile))
                    copy(rows(region, tile + base), ps[:, 4 + b, :], post_gain(s)[:, ds(tile, 1)]).then_inc(u_ready, 1)
                    act.wait_ge(post_summed, tile + ((DK + 1) * s + 1))
                    nc.scalar.activation(square[b][:, :], ps[:, 4 + b, :], ACT.Square).then_inc(post_square, 1)

                split_then(name, per_tile, take)

            def ffn(f, s):
                def take(tile, b):
                    act.wait_ge(gate_scaled, tile + (FT * f + 1))
                    nc.scalar.activation(scaled[b][:, :], scaled[b][:, :], ACT.Silu).then_inc(silu_done, 1)
                    act.wait_ge(a_ready, tile + (FT * f + 1))
                    copy(rows_r(a_hi, tile), scaled[b][:, :]).then_inc(a_hi_ready, 1)

                split_then(f"gate_up{f}", 2, take)
                take_out(s, f"down{f}", 2)

            def silu_rows(name, first_tile, base, first_row):
                def take(tile, n):
                    act.wait_ge(tile_taken, tile + (first_tile + 1))
                    nc.scalar.activation(rows(a_rows, tile + base), scaled[n % 2][:, :], ACT.Silu).then_inc(row_silu, 1)
                split_then(name, 1, take)

            def even():
                s = EVEN
                split_then("qk_small", 1, lambda tile, n: None)
                split_then("v", 1, lambda tile, n: None)
                for h in range(GH):
                    act.wait_ge(logit_ready, h + 1)
                    after(nc.scalar.activation(other[h % 2][:, :], other[h % 2][:, :], ACT.Exp, scale=-1.0))
                    nc.scalar.activation(other[h % 2][:, :], other[h % 2][:, :], ACT.Ln, bias=1.0).then_inc(softplus_ready, 1)
                silu_rows("g", G0, CAT, 0)
                act.wait_ge(log_a_ready, GH)
                with act.Fori(0, GH) as h:
                    log_a = rows(a_rows, h + LOG_A)
                    copy(v_head, rows(a_rows, V, 8).rearrange("p (c v) -> p c v", c=NC)[:, :, ds(h * GDV, GDV)]).then_inc(value_copied, 1)
                    for j in range(len(SPANS)):
                        act.wait_ge(gla_diff, h * 8 + (j + 1))
                        nc.scalar.activation(scaled[j % 2][:, :], scaled[j % 2][:, :], ACT.Exp).then_inc(gla_decay, 1)
                    act.wait_ge(gla_products, h * 9 + 6)
                    copy(k_dec[1], rows(a_rows, h + K)).then_inc(key_copied, 1)
                    act.wait_ge(gla_factors, h * 8 + 6)
                    nc.scalar.activation(scaled[1][:, P:T], log_a[:, P:T], ACT.Exp)
                    nc.scalar.activation(chunk_decay, log_a[:, P - 1:T:P], ACT.Exp)
                    act.wait_ge(gla_diff, h * 8 + 8)
                    nc.scalar.activation(scaled[0][:, 0:3 * P], scaled[0][:, 0:3 * P], ACT.Exp).then_inc(gla_decay, 1)
                    act.wait_ge(gla_products, h * 9 + 9)
                    copy(scores[:, 0, 1:4, :], ps[:, 2, 0:3 * P].rearrange("p (i t) -> p i t", t=P))
                    copy(scores[:, 1, 2:4, :], ps[:, 3, 0:2 * P].rearrange("p (i t) -> p i t", t=P))
                    copy(scores[:, 2, 3:4, :], ps[:, 3, 2 * P:3 * P].rearrange("p (i t) -> p i t", t=P)).then_inc(far_taken, 1)
                    act.wait_ge(gla_out, h + 1)
                    nc.scalar.activation(square_sum[:, :], ps[:, 4, :], ACT.Square)
                    nc.scalar.activation(gated, ps[:, 5, :], ACT.Square).then_inc(head_squares, 1)
                silu_rows("z", Z0, CAT + 8, 0)

                def take_conv(tile, n):
                    act.wait_ge(conv_done, tile + 1)
                    nc.scalar.activation(rows(a_rows, tile + XS), scaled[n % 2][:, :], ACT.Silu).then_inc(row_silu, 1)
                split_then("xbc", 1, take_conv)

                act.wait_ge(dt_signal, 1)
                nc.scalar.activation(far1, far1, ACT.Exp, scale=-1.0)
                nc.scalar.activation(a_log, a_log, ACT.Exp).then_inc(dt_act, 1)
                act.wait_ge(dt_signal, 2)
                nc.scalar.activation(cum, far2, ACT.Ln).then_inc(dt_act, 1)
                act.wait_ge(dt_cum, 1)
                nc.scalar.activation(ssm_chunk_decay, cum[:, P - 1:T:P], ACT.Exp)
                act.wait_ge(dt_cum, 2)
                nc.scalar.activation(far1[:, 0:3 * P], far1[:, 0:3 * P], ACT.Exp).then_inc(dt_act, 1)

                with act.Fori(0, SG) as g:
                    copy(b_group, rows(a_rows, g + B_ROWS))
                    copy(rows(h_rows, 14, 2), rows(a_rows, g * 2 + XS, 2)).then_inc(group_copied, 1)
                    act.wait_ge(cb_ready, g + 1)
                    copy(cb[:, 0, 1:4, :], ps[:, 2, P:T].rearrange("p (i t) -> p i t", t=P))
                    copy(cb[:, 1, 2:4, :], ps[:, 3, 2 * P:T].rearrange("p (i t) -> p i t", t=P))
                    copy(cb[:, 2, 3:4, :], ps[:, 4, 3 * P:T].rearrange("p (i t) -> p i t", t=P)).then_inc(cb_far_taken, 1)
                    for r in range(4):
                        half = slice(64 * (r % 2), 64 * (r % 2) + 64)
                        act.wait_ge(row_spread, g * 4 + (r + 1))
                        nc.scalar.activation(from_start[r // 2][half, :], ps[half, r % 2, :], ACT.Exp).then_inc(from_start_ready, 1)
                        act.wait_ge(decay_diff, g * 4 + (r + 1))
                        nc.scalar.activation(decay[r % 2], decay[r % 2], ACT.Exp).then_inc(decay_exp, 1)
                    act.wait_ge(y_gated, g * 2 + 1)
                    nc.scalar.activation(square_sum[:, :], rows(a_rows, g * 2 + (CAT + 8)), ACT.Square)
                    act.wait_ge(y_gated, g * 2 + 2)
                    nc.scalar.activation(other[0][:, :], rows(a_rows, g * 2 + (CAT + 9)), ACT.Square).then_inc(group_squares, 1)
                act.wait_ge(group_done, SG)
                for n in range(4):
                    copy(cat_hi[:, 4 * n:4 * n + 4, :], a_rows[:, CAT + 4 * n:CAT + 4 * n + 4, :]).then_inc(cat_hi_ready, 1)
                take_out(s, "even_out", 2)

            def odd():
                s = ODD
                split_then("latent", 1, lambda tile, n: None)
                act.wait_ge(tile_taken, LATENT0 + QR)
                for n in range(QR):
                    nc.scalar.activation((square_sum, *other)[n][:, :], rows(a_rows, LATENT + n), ACT.Square).then_inc(latent_square, 1)
                for n in range(QR):
                    act.wait_ge(latent_normed, n + 1)
                    copy(latent_hi[:, n, :], rows(a_rows, LATENT + n)).then_inc(latent_hi_ready, 1)
                for n in range(KR):
                    nc.scalar.activation((square_sum, *other)[n][:, :], rows(a_rows, LATENT + QR + n), ACT.Square).then_inc(latent_square, 1)
                for n in range(QR, QR + KR):
                    act.wait_ge(latent_normed, n + 1)
                    copy(latent_hi[:, n, :], rows(a_rows, LATENT + n)).then_inc(latent_hi_ready, 1)

                def take_q(tile, n):
                    act.wait_ge(slot_done, stages["q_up"][0] + tile + 1)
                    for m, row in enumerate((QN + 2 * tile, QN + 2 * tile + 1, QROPE + tile)):
                        copy(rows(a_rows, row), ps[:, 3 * (tile % 2) + m, :]).then_inc(q_taken, 1)
                split_then("q_up", 1, take_q)
                for n in range(2):
                    act.wait_ge(angle_ready, n + 1)
                    nc.scalar.activation((sin, cos)[n], angle[1], ACT.Sin).then_inc(table_ready, 1)
                split_then("k_up", 1, lambda tile, n: None)

                def take_v(tile, n):
                    act.wait_ge(slot_done, stages["v_up"][0] + tile + 1)
                    act.wait_ge(rope_done, 1)
                    for c in range(NC):
                        copy(rows(a_rows, VT + 2 * c + tile), ps[:, c, :]).then_inc(v_taken, 1)
                split_then("v_up", 1, take_v)

                act.wait_ge(v_taken, 2 * NC)
                act.wait_ge(rope_done, 1 + MH // 2)
                with act.Fori(0, MH // 2) as i:
                    copy(q_pair, rows(a_rows, i + QROPE))
                    copy(v_pair, rows(a_rows, VT, 8).rearrange("p (c v) -> p c v", c=NC)[:, :, ds(i * 256, 256)]).then_inc(pair_copied, 1)
                    for e in range(2):
                        if e:
                            act.wait_ge(scores_done, i * 8 + 4)
                        copy(q_head, rows(a_rows, i * 2 + (QN + e))).then_inc(q_copied, 1)
                        for qt in range(NC):
                            act.wait_ge(bias_ready, i * 2 + (e + 1))
                            nc.scalar.activation(probs[:, qt, 0:(qt + 1) * P], ps[:, qt, 0:(qt + 1) * P], ACT.Exp,
                                                 bias=peak_bias[:, qt:qt + 1], scale=SCORE_SCALE,
                                                 accum_out=prob_sum[:, qt:qt + 1]).then_inc(exp_done, 1)
                        for kc in (1, 3):
                            act.wait_ge(probs_turned, i * 8 + (4 * e + kc + 1))
                            copy(probs_t[:, kc, kc * P:T], ps[:, 4 + kc % 2, kc * P:T]).then_inc(turned_act, 1)
                        act.wait_ge(att_done, i * 2 + (e + 1))
                        copy(rows_r(o_hi, i * 2 + e), ps[:, 6 + e, :]).then_inc(o_hi_ready, 1)
                take_out(s, "odd_out", 1)

            act.wait_ge(consts_in, 48)
            act.wait_ge(x_in, 16)
            for n in range(RING):
                split_high(n, 0, width_of(n))
            act.wait_ge(gains_halved, 1)
            for s in range(N_SUB):
                if s == EVEN:
                    act.dma_start(rows(a_rows, 14, 2), dram["level_mask"]).then_inc(even_in, 16)
                    act.dma_start(tri, dram["tri"]).then_inc(even_in, 16)
                    act.dma_start(gate2, dram["gate2"]).then_inc(even_in, 16)
                if s == ODD:
                    act.dma_start(angle[0].bitcast(I32), dram["positions"].to_broadcast([P, T])).then_inc(odd_in, 16)
                    act.dma_start(causal, dram["causal"]).then_inc(odd_in, 16)
                    act.dma_start(turn_mat, dram["turn"]).then_inc(odd_in, 16)
                pre_norm(s)
                if s == EVEN:
                    even()
                elif s == ODD:
                    odd()
                else:
                    ffn(FFN_OF[s], s)

        @block.tensor
        def _(pe):
            def products(bank, slot, column, hi, lo, first, last):
                w_h = w_hi[slot % RING][:, column:column + P]
                w_l = w_lo[slot % RING][:, column:column + P]
                nc.tensor.matmul(ps[:, bank, :], w_h, hi, start=first, stop=False)
                nc.tensor.matmul(ps[:, bank, :], w_h, lo, start=False, stop=False)
                return nc.tensor.matmul(ps[:, bank, :], w_l, hi, start=False, stop=last)

            def slot_ready(slot, turns=0):
                pe.wait_ge(hi_done, slot + 1 + turns)
                pe.wait_ge(lo_done, slot + 1 + turns)

            def norm_sums(source_summed, count):
                pe.wait_ge(source_summed, count)
                for c in range(NC):
                    last = nc.tensor.matmul(ps[:, SUMS, c:c + 1], square_sum[:, c * P:c * P + P], ones[:, 0:1], start=True, stop=True)
                last.then_inc(sums_ready, 1)

            def norm_spread(n):
                pe.wait_ge(diag_ready, n + 1)
                nc.tensor.matmul(ps[:, SPREAD, :], ones[:, :], other[1][:, :], start=True, stop=True).then_inc(spread_ready, 1)

            def first_four(s, name, bank0):
                first = stages[name][0]
                for m in range(RING):
                    slot_ready(first + m)
                for k in range(DK):
                    pe.wait_ge(h_lo_ready, DK * s + k + 1)
                    if k == DK - 1:
                        norm_sums(pre_summed, (DK - 1) * (s + 1))
                    for m in range(RING):
                        last = products((bank0 + m) % 4, first + m, k * P, h_hi[:, k, :], h_lo[:, k, :], k == 0, k == DK - 1)
                        if k == DK - 1:
                            last.then_inc(slot_done, 1)
                norm_spread(norms[(s, "pre")])

            def sublayer_out(s, name, per_tile, blocks, source, source_ready):
                first = stages[name][0]
                per_turn = 4 // per_tile

                def tile(n, turn, fresh):
                    if s or not fresh or n > 1:
                        pe.wait_ge(post_square, turn * per_turn + (DK * s + n - 1))
                    for m in range(per_tile):
                        slot = first + n * per_tile + m
                        slot_ready(slot, turn * 4)
                        for k in range(blocks):
                            kk = m * blocks + k
                            if fresh and n == 0:
                                source_ready(kk)
                            hi, lo = source(kk)
                            last = products(4 + n % 2, slot, k * P, hi, lo, kk == 0, kk == per_tile * blocks - 1)
                        last.then_inc(slot_done, 1)

                for n in range(per_turn):
                    tile(n, 0, True)
                with pe.Fori(1, DK // per_turn) as turn:
                    for n in range(per_turn):
                        tile(n, turn, False)
                norm_sums(post_summed, (DK + 1) * (s + 1))
                norm_spread(norms[(s, "post")])

            def ffn(f, s):
                name = f"gate_up{f}"
                first = stages[name][0]
                first_four(s, name, 0)
                with pe.Fori(1, FT // 2) as turn:
                    for m in range(4):
                        if m % 2 == 0:
                            pe.wait_ge(up_scaled, turn * 2 + (FT * f + m // 2 - 1))
                        slot_ready(first + m, turn * 4)
                        for k in range(DK):
                            last = products(m, first + m, k * P, h_hi[:, k, :], h_lo[:, k, :], k == 0, k == DK - 1)
                        last.then_inc(slot_done, 1)
                sublayer_out(s, f"down{f}", 2, HALF, lambda k: (a_hi[:, k, :], a_lo[:, k, :]),
                             lambda k: pe.wait_ge(a_lo_ready, FT * f + k + 1))

            def projection(name, first_tile, done=0):
                first, slots, _ = stages[name]

                def tile(n, turns):
                    bank = (first_tile + n) % 4
                    slot_ready(first + n, turns * 4)
                    pe.wait_ge(tile_taken, turns * 4 + (first_tile + n - 3))
                    for k in range(DK):
                        last = products(bank, first + n, k * P, h_hi[:, k, :], h_lo[:, k, :], k == 0, k == DK - 1)
                    last.then_inc(slot_done, 1)

                turns = (slots - done) // 4
                if turns > 1:
                    with pe.Fori(0, turns) as turn:
                        for n in range(4):
                            tile(done + n, turn)
                else:
                    turns = 0
                for n in range(done + 4 * turns, slots):
                    tile(n, 0)

            def even():
                s = EVEN
                first_four(s, "qk_small", QK0)
                projection("qk_small", QK0, 4)
                first = stages["v"][0]
                with pe.Fori(0, 2) as half:
                    for n in range(4):
                        slot_ready(first + n, half * 4)
                        slot = (first + n) % RING
                        for m in range(2):
                            k = 2 * n + m
                            w_h, w_l = w_hi[slot][:, m * T:m * T + T], w_lo[slot][:, m * T:m * T + T]
                            for c in range(NC):
                                bank = (V0 + c) % 4
                                if k == 0:
                                    pe.wait_ge(tile_taken, half * 4 + (V0 + c - 3))
                                h_h, h_l = h_hi[:, k, c * P:c * P + P], h_lo[:, k, c * P:c * P + P]
                                nc.tensor.matmul(ps[:, bank, :], h_h, w_h, start=k == 0, stop=False)
                                nc.tensor.matmul(ps[:, bank, :], h_h, w_l, start=False, stop=False)
                                last = nc.tensor.matmul(ps[:, bank, :], h_l, w_h, start=False, stop=k == DK - 1)
                        last.then_inc(slot_done, 1)
                pe.wait_ge(even_in, 48)
                pe.wait_ge(tile_taken, QK0 + 9)
                for h in range(GH):
                    last = nc.tensor.matmul(ps[:, 4 + h, :], gate2[:, h * P:h * P + P], small[0:RANK, :], start=True, stop=True)
                last.then_inc(decay_logits, 1)
                projection("g", G0)
                gla_heads()
                projection("z", Z0)
                projection("xbc", XBC0)
                ssm_groups()
                sublayer_out(s, "even_out", 2, 8, lambda k: (cat_hi[:, k, :], cat_lo[:, k, :]),
                             lambda k: pe.wait_ge(cat_lo_ready, k // 4 + 1))

            def gla_heads():
                with pe.Fori(0, GH) as h:
                    for j in range(len(SPANS)):
                        pe.wait_ge(gla_factors, h * 8 + (j + 1))
                        if j >= 2:
                            pe.wait_ge(gla_merged, h * 8 + (j - 1))
                        for c in range(NC):
                            cols = slice(c * P, c * P + P)
                            last = nc.tensor.matmul(ps[:, j % 2, cols], k_dec[j % 2][:, cols], other[j % 2][:, cols], start=True, stop=True)
                        last.then_inc(gla_products, 1)
                    pe.wait_ge(key_copied, h + 1)
                    pe.wait_ge(gla_merged, h * 8 + 6)
                    q = rows(a_rows, h + Q)
                    for c in range(NC):
                        cols = slice(c * P, c * P + P)
                        last = nc.tensor.matmul(ps[:, 1, cols], k_dec[1][:, cols], q[:, cols], start=True, stop=True)
                    last.then_inc(gla_products, 1)
                    pe.wait_ge(gla_factors, h * 8 + 8)
                    for (jc, ic) in FAR:
                        key = {1: k_dec[0][:, jc * P:jc * P + P], 2: k_dec[1][:, jc * P:jc * P + P], 3: k_dec[1][:, 2 * P:3 * P]}[ic - jc]
                        bank, at = ((2, ic - 1) if jc == 0 else (3, ic - 2 if jc == 1 else 2))
                        last = nc.tensor.matmul(ps[:, bank, at * P:at * P + P], key, other[0][:, ic * P:ic * P + P], start=True, stop=True)
                    last.then_inc(gla_products, 1)
                    pe.wait_ge(gla_merged, h * 8 + 8)
                    pe.wait_ge(far_taken, h + 1)
                    pe.wait_ge(value_copied, h + 1)
                    for m in range(2):
                        for jc in range(NC):
                            last = nc.tensor.matmul(ps[:, 4 + m, jc * P:T], v_head[:, jc, m * P:m * P + P],
                                                    scores[:, jc, jc:NC, :].rearrange("p i t -> p (i t)"), start=jc == 0, stop=jc == NC - 1)
                    last.then_inc(gla_out, 1)
                    norm_sums(head_summed, h + 1)
                    norm_spread(h + norms[("gla", 0)])

            def ssm_groups():
                pe.wait_ge(dt_far, 1)
                for n in range(14):
                    if n < 8:
                        source = (dt_rows if n < 4 else cum)[:, (n % 4) * P:(n % 4) * P + P]
                    else:
                        jc, ic = FAR[n - 8]
                        source = {1: far1[:, jc * P:jc * P + P], 2: far2[:, jc * P:jc * P + P], 3: far2[:, 2 * P:3 * P]}[ic - jc]
                    last = nc.tensor.matmul(ps[:, 4, n * SH:n * SH + SH], source, ident[DT0:DT0 + SH, DT0:DT0 + SH], start=True, stop=True)
                last.then_inc(cols_turned, 1)
                pe.wait_ge(cols_ready, 1)
                with pe.Fori(0, SG) as g:
                    pe.wait_ge(group_copied, g + 1)
                    for c in range(NC):
                        for m in range(2):
                            at = ((c % 2) * 2 + m) * P
                            last = nc.tensor.transpose(ps[:, c // 2, at:at + P], xs_group[:, m, c * P:c * P + P], ident[:, :])
                    last.then_inc(x_turned, 1)
                    c_row = rows(a_rows, g + C_ROWS)
                    for jc in range(NC):
                        last = nc.tensor.matmul(ps[:, 2 + jc, jc * P:T], b_group[:, jc * P:jc * P + P], c_row[:, jc * P:T], start=True, stop=True)
                    last.then_inc(cb_ready, 1)

                    def spread_row(r):
                        pe.wait_ge(head_row_ready, g * 4 + (r + 1))
                        if r < 2:
                            pe.wait_ge(x_taken, g + 1)
                        else:
                            pe.wait_ge(decay_diff, g * 4 + (r - 1))
                            pe.wait_ge(from_start_ready, g * 4 + (r - 1))
                        nc.tensor.matmul(ps[:, r % 2, :], ones[DT0:DT0 + SH, :], head_row[r % 2], start=True, stop=True).then_inc(row_spread, 1)

                    def near(r):
                        pe.wait_ge(decay_ready, g * 4 + (r + 1))
                        half = slice(64 * (r % 2), 64 * (r % 2) + 64)
                        for c in range(NC):
                            cols = slice(c * P, c * P + P)
                            last = nc.tensor.matmul(ps[half, 2 + r // 2, cols], x_group[:, c, r * 64:r * 64 + 64], decay[r % 2][:, cols],
                                                    start=True, stop=True)
                        last.then_inc(y_diag_done, 1)

                    spread_row(0)
                    spread_row(1)
                    pe.wait_ge(cb_far_taken, g + 1)
                    pe.wait_ge(x_far_ready, g + 1)
                    near(0)
                    spread_row(2)
                    near(1)
                    spread_row(3)
                    for m in range(2):
                        for ic in range(1, NC):
                            for jc in range(ic):
                                last = nc.tensor.matmul(ps[:, 4 + m, ic * P:ic * P + P], x_far[:, FAR.index((jc, ic)), m * P:m * P + P],
                                                        cb[:, jc, ic, :], start=jc == 0, stop=jc == ic - 1)
                    last.then_inc(y_far_done, 1)
                    near(2)
                    near(3)
                    norm_sums(group_summed, g + 1)
                    norm_spread(g + norms[("ssm", 0)])

            def odd():
                s = ODD
                first_four(s, "latent", LATENT0)
                projection("latent", LATENT0, 4)
                norm_sums(latent_summed, 1)
                norm_spread(norms["q_latent"])
                norm_sums(latent_summed, 2)
                norm_spread(norms["kv_latent"])

                def turn(j):
                    if j == 0:
                        pe.wait_ge(tile_taken, LATENT0 + 6)
                        pe.wait_ge(odd_in, 48)
                    else:
                        pe.wait_ge(q_taken, 3 * j)
                        pe.wait_ge(rope_taken, j)
                    source = rows(a_rows, LATENT + 5 if j == 0 else QROPE + j - 1)
                    nc.tensor.matmul(ps[:, 7, :], turn_mat, source, start=True, stop=True).then_inc(rope_turned, 1)

                first = stages["q_up"][0]
                for i in range(MH // 2):
                    slot_ready(first + i)
                    if i >= 2:
                        pe.wait_ge(q_taken, 3 * (i - 1))
                    for m in range(3):
                        for k in range(QR):
                            pe.wait_ge(latent_lo_ready, k + 1)
                            last = products(3 * (i % 2) + m, first + i, (3 * m + k) * P, latent_hi[:, k, :], latent_lo[:, k, :], k == 0, k == QR - 1)
                    last.then_inc(slot_done, 1)
                first = stages["k_up"][0]
                pe.wait_ge(latent_lo_ready, QR + KR)
                for i in range(2):
                    slot_ready(first + i)
                    for m in range(4):
                        pe.wait_ge(q_taken, 12) if i == 0 else pe.wait_ge(k_taken, m + 1)
                        for k in range(KR):
                            last = products(m, first + i, (2 * m + k) * P, latent_hi[:, QR + k, :], latent_lo[:, QR + k, :], k == 0, k == KR - 1)
                    last.then_inc(slot_done, 1)
                turn(0)
                first = stages["v_up"][0]
                for i in range(2):
                    slot_ready(first + i)
                    slot = (first + i) % RING
                    for c in range(NC):
                        pe.wait_ge(k_taken, 5 + c) if i == 0 else pe.wait_ge(v_taken, c + 1)
                        for k in range(KR):
                            w_h, w_l = w_hi[slot][:, k * T:k * T + T], w_lo[slot][:, k * T:k * T + T]
                            l_h, l_l = latent_hi[:, QR + k, c * P:c * P + P], latent_lo[:, QR + k, c * P:c * P + P]
                            nc.tensor.matmul(ps[:, c, :], l_h, w_h, start=k == 0, stop=False)
                            nc.tensor.matmul(ps[:, c, :], l_h, w_l, start=False, stop=False)
                            last = nc.tensor.matmul(ps[:, c, :], l_l, w_h, start=False, stop=k == KR - 1)
                    last.then_inc(slot_done, 1)
                    turn(i + 1)
                turn(3)
                turn(4)

                pe.wait_ge(v_taken, 2 * NC)
                pe.wait_ge(rope_done, 5)
                with pe.Fori(0, MH // 2) as i:
                    pe.wait_ge(pair_copied, i + 1)
                    for e in range(2):
                        half = slice(64 * e, 64 * e + 64)
                        k_row = rows(a_rows, i * 2 + (KN + e))
                        pe.wait_ge(q_copied, i * 2 + (e + 1))
                        for qt in range(NC):
                            n = (qt + 1) * P
                            nc.tensor.matmul(ps[:, qt, 0:n], q_head[:, qt * P:qt * P + P], k_row[:, 0:n], start=True, stop=False)
                            nc.tensor.matmul(ps[:, qt, 0:n], q_pair[half, qt * P:qt * P + P], krope[half, 0:n],
                                             start=False, stop=True).then_inc(scores_done, 1)
                        pe.wait_ge(probs_ready, i * 2 + (e + 1))
                        for kc in range(NC):
                            if kc >= 2:
                                pe.wait_ge(turned_dve if kc == 2 else turned_act, i * 4 + (2 * e + 1))
                            for qt in range(kc, NC):
                                last = nc.tensor.transpose(ps[:, 4 + kc % 2, qt * P:qt * P + P], probs[:, qt, kc * P:kc * P + P], ident[:, :])
                            last.then_inc(probs_turned, 1)
                        pe.wait_ge(turned_dve, i * 4 + (2 * e + 2))
                        pe.wait_ge(turned_act, i * 4 + (2 * e + 2))
                        for kc in range(NC):
                            last = nc.tensor.matmul(ps[:, 6 + e, kc * P:T], v_pair[:, kc, e * P:e * P + P], probs_t[:, kc, kc * P:T],
                                                    start=kc == 0, stop=kc == NC - 1)
                        last.then_inc(att_done, 1)
                sublayer_out(s, "odd_out", 1, 8, lambda k: (o_hi[:, k, :], o_lo[:, k, :]),
                             lambda k: pe.wait_ge(o_lo_ready, k + 1))

            pe.wait_ge(consts_in, 48)
            pe.wait_ge(consts_made, 2)
            for s in range(N_SUB):
                if s == EVEN:
                    even()
                elif s == ODD:
                    odd()
                else:
                    ffn(FFN_OF[s], s)

        @block.vector
        def _(dve):
            steps, offset = [0], [None]

            def signal(ins):
                steps[0] += 1
                ins.then_inc(dve_step, 1)

            def settle():
                dve.wait_ge(dve_step, steps[0] if offset[0] is None else offset[0] + steps[0])

            def after(ins):
                signal(ins)
                settle()

            @contextmanager
            def loop(turns, per_turn):
                before = steps[0]
                with dve.Fori(0, turns) as turn:
                    offset[0] = turn * per_turn
                    yield turn
                offset[0] = None
                assert steps[0] - before == per_turn, steps[0] - before
                steps[0] = before + per_turn * turns

            def tt(to, a, b, op):
                return nc.vector.tensor_tensor(to, a, b, op)

            def ts(to, a, s1, s2, op0, op1=ALU.bypass):
                return nc.vector.tensor_scalar(to, a, s1, s2, op0, op1) if s2 is not None else nc.vector.tensor_scalar(to, a, s1, None, op0)

            def stt(to, a, scalar, b, op0, op1):
                return nc.vector.scalar_tensor_tensor(out=to, in0=a, scalar=scalar, in1=b, op0=op0, op1=op1)

            def norm(n, columns, to=rstd[:, :]):
                dve.wait_ge(sums_ready, n + 1)
                ts(mean[:, :], ps[:, SUMS, 0:NC], 1.0 / columns, EPS, ALU.mult, ALU.add).then_inc(mean_ready, 1)
                dve.wait_ge(rstd_col_ready, n + 1)
                for c in range(NC):
                    last = ts(diag[:, c, :], ident[:, :], rstd_col[:, c:c + 1], None, ALU.mult)
                last.then_inc(diag_ready, 1)
                dve.wait_ge(spread_ready, n + 1)
                nc.vector.tensor_copy(to, ps[:, SPREAD, :]).then_inc(rstd_ready, 1)
                dve.wait_ge(rstd_ready, n + 1)

            def add_update(s, k):
                dve.wait_ge(u_ready, DK * (s + 1))
                after(tt(scaled[k % 2][:, :], u_row(s, k), rstd[:, :], ALU.mult))
                tt(x[:, k, :], x[:, k, :], scaled[k % 2][:, :], ALU.add).then_inc(residual_ready, 1)

            def low_of_h(s, k):
                dve.wait_ge(h_hi_ready, DK * s + k + 1)
                stt(h_lo[:, k, :], x[:, k, :], pre_gain(s)[:, k:k + 1], h_hi[:, k, :].bitcast(F32),
                    ALU.mult, ALU.subtract).then_inc(h_lo_ready, 1)

            def pre_norm(s):
                for k in range(DK):
                    if s:
                        add_update(s - 1, k)
                    if k:
                        low_of_h(s, k - 1)
                low_of_h(s, DK - 1)
                norm(norms[(s, "pre")], D)

            def post_norm(s):
                nc.vector.memset(square_sum[:, :], 0.0).then_inc(post_summed, 1)
                for tile in range(DK):
                    dve.wait_ge(post_square, DK * s + tile + 1)
                    dve.wait_ge(post_summed, (DK + 1) * s + tile + 1)
                    tt(square_sum[:, :], square_sum[:, :], square[tile % 2][:, :], ALU.add).then_inc(post_summed, 1)
                norm(norms[(s, "post")], D)

            def ffn(f, s):
                slot = stages[f"gate_up{f}"][0]

                def take(tile, b):
                    dve.wait_ge(slot_done, tile * 2 + (slot + 1))
                    tt(scaled[b][:, :], ps[:, 2 * b, :], rstd[:, :], ALU.mult).then_inc(gate_scaled, 1)
                    dve.wait_ge(slot_done, tile * 2 + (slot + 2))
                    tt(other[b][:, :], ps[:, 2 * b + 1, :], rstd[:, :], ALU.mult).then_inc(up_scaled, 1)
                    dve.wait_ge(silu_done, tile + (FT * f + 1))
                    dve.wait_ge(up_scaled, tile + (FT * f + 1))
                    tt(scaled[b][:, :], scaled[b][:, :], other[b][:, :], ALU.mult).then_inc(a_ready, 1)
                    dve.wait_ge(a_hi_ready, tile + (FT * f + 1))
                    tt(rows_r(a_lo, tile), scaled[b][:, :], rows_r(a_hi, tile).bitcast(F32), ALU.subtract).then_inc(a_lo_ready, 1)

                with dve.Fori(0, FT // 2) as turn:
                    for b in range(2):
                        take(turn * 2 + b, b)
                post_norm(s)

            def even():
                s = EVEN
                slot = stages["qk_small"][0]
                for n in range(9):
                    dve.wait_ge(slot_done, slot + n + 1)
                    source = ps[:, (QK0 + n) % 4, :]
                    if n < GH:
                        stt(rows(a_rows, Q + n), source, float(P) ** -0.5, rstd[:, :], ALU.mult, ALU.mult).then_inc(tile_taken, 1)
                    else:
                        tt(rows(a_rows, K + n - GH) if n < 2 * GH else small, source, rstd[:, :], ALU.mult).then_inc(tile_taken, 1)
                slot = stages["v"][0]
                for half in range(2):
                    dve.wait_ge(slot_done, slot + 4 * half + 4)
                    for c in range(NC):
                        ts(rows(a_rows, V + 2 * c + half), ps[:, (V0 + c) % 4, :], rstd_col[:, c:c + 1], None, ALU.mult).then_inc(tile_taken, 1)

                dve.wait_ge(decay_logits, 1)
                for h in range(GH):
                    row = rows(a_rows, LOG_A + h)
                    after(ts(row, ps[:, 4 + h, :], gla_bias[:, h:h + 1], None, ALU.add))
                    if h >= 2:
                        dve.wait_ge(softplus_ready, h - 1)
                        after(stt(rows(a_rows, LOG_A + h - 2), rows(a_rows, LOG_A + h - 2), 0.0, other[h % 2][:, :], ALU.min, ALU.subtract))
                    stt(other[h % 2][:, :], row, -1.0, row, ALU.mult, ALU.max).then_inc(logit_ready, 1)
                for h in (2, 3):
                    dve.wait_ge(softplus_ready, h + 1)
                    after(stt(rows(a_rows, LOG_A + h), rows(a_rows, LOG_A + h), 0.0, other[h % 2][:, :], ALU.min, ALU.subtract))
                after(ts(rows(a_rows, LOG_A, 4), rows(a_rows, LOG_A, 4), 1.0 / 16.0, None, ALU.mult))
                for h in range(GH):
                    for c in range(NC):
                        part = rows(a_rows, LOG_A + h)[:, c * P:c * P + P]
                        last = nc.vector.tensor_tensor_scan(part, ones[:, :], part, 0.0, ALU.mult, ALU.add)
                    last.then_inc(log_a_ready, 1)
                scale_rows("g", G0, 0)
                gla_heads()
                scale_rows("z", Z0, 8)

                for b in range(2):
                    last = nc.vector.memset(pad[b][:, 0:3], 0.0)
                after(last)
                slot = stages["xbc"][0]
                with loop(4, 4 * 3) as turn:
                    for n in range(4):
                        b = n % 2
                        dve.wait_ge(slot_done, turn * 4 + (slot + n + 1))
                        tt(pad[b][:, 3:T + 3], ps[:, (XBC0 + n) % 4, :], rstd[:, :], ALU.mult).then_inc(tile_taken, 1)
                        dve.wait_ge(tile_taken, turn * 4 + (XBC0 + n + 1))
                        dve.wait_ge(row_silu, turn * 4 + (16 + n - 1))
                        w = mixer_cols[:, ds(turn * 16 + 4 * n, 4)]
                        after(ts(scaled[b][:, :], pad[b][:, 0:T], w[:, 0:1], mixer_cols[:, ds(turn * 4 + (64 + n), 1)], ALU.mult, ALU.add))
                        after(stt(scaled[b][:, :], pad[b][:, 1:T + 1], w[:, 1:2], scaled[b][:, :], ALU.mult, ALU.add))
                        after(stt(scaled[b][:, :], pad[b][:, 2:T + 2], w[:, 2:3], scaled[b][:, :], ALU.mult, ALU.add))
                        stt(scaled[b][:, :], pad[b][:, 3:T + 3], w[:, 3:4], scaled[b][:, :], ALU.mult, ALU.add).then_inc(conv_done, 1)
                dve.wait_ge(row_silu, 32)
                ssm_groups()
                for n in range(4):
                    dve.wait_ge(cat_hi_ready, n + 1)
                    tt(cat_lo[:, 4 * n:4 * n + 4, :], a_rows[:, CAT + 4 * n:CAT + 4 * n + 4, :],
                       cat_hi[:, 4 * n:4 * n + 4, :].bitcast(F32), ALU.subtract).then_inc(cat_lo_ready, 1)
                post_norm(s)

            def scale_rows(name, first_tile, first_silu):
                slot = stages[name][0]
                for n in range(8):
                    dve.wait_ge(slot_done, slot + n + 1)
                    if n >= 2 or first_silu:
                        dve.wait_ge(row_silu, first_silu + n - 1)
                    tt(scaled[n % 2][:, :], ps[:, (first_tile + n) % 4, :], rstd[:, :], ALU.mult).then_inc(tile_taken, 1)

            def gla_heads():
                diagonal_scores = diagonal(scores)
                dve.wait_ge(even_in, 48)
                nc.vector.tensor_copy(level_mask.rearrange("p l t -> p (l t)"), rows(a_rows, 14, 2))
                after(nc.vector.memset(rows(a_rows, 8, 4), 0.0))
                dve.wait_ge(row_silu, 8)
                with loop(GH, 5) as h:
                    log_a, q, k = rows(a_rows, h + LOG_A), rows(a_rows, h + Q), rows(a_rows, h + K)

                    def differences(j):
                        span = SPANS[j]
                        blocks = log_a.rearrange("p (n w t) -> p n w t", w=2, t=span)
                        to = scaled[j % 2][:, :].rearrange("p (n w t) -> p n w t", w=2, t=span)
                        if j >= 2:
                            dve.wait_ge(gla_factors, h * 8 + (j - 1))
                        middle = blocks[:, :, 0, span - 1:span].to_broadcast([P, T // (2 * span), span])
                        tt(to[:, :, 0, :], middle, blocks[:, :, 0, :], ALU.subtract)
                        tt(to[:, :, 1, :], blocks[:, :, 1, :], middle, ALU.subtract).then_inc(gla_diff, 1)

                    def factors(j):
                        dve.wait_ge(gla_decay, h * 8 + (j + 1))
                        if j >= 2:
                            dve.wait_ge(gla_products, h * 9 + (j - 1))
                        if j >= 3:
                            dve.wait_ge(gla_merged, h * 8 + (j - 2))
                        tt(other[j % 2][:, :], q, scaled[j % 2][:, :], ALU.mult)
                        tt(k_dec[j % 2], k, scaled[j % 2][:, :], ALU.mult).then_inc(gla_factors, 1)

                    def merge(j):
                        nc.vector.copy_predicated(diagonal_scores, level_mask[:, j:j + 1, :].to_broadcast([P, NC, P]),
                                                  ps[:, j % 2, :].rearrange("p (c t) -> p c t", c=NC)).then_inc(gla_merged, 1)

                    for j in range(len(SPANS) + 1):
                        if j < len(SPANS):
                            differences(j)
                        if j:
                            factors(j - 1)
                        if j == len(SPANS):
                            chunks = log_a.rearrange("p (c t) -> p c t", c=NC)[:, 0:3, :]
                            dve.wait_ge(gla_factors, h * 8 + 7)
                            tt(scaled[0][:, 0:3 * P].rearrange("p (c t) -> p c t", c=3), chunks[:, :, P - 1:P].to_broadcast([P, 3, P]),
                               chunks, ALU.subtract).then_inc(gla_diff, 1)
                        if j >= 3:
                            merge(j - 3)
                    dve.wait_ge(gla_decay, h * 8 + 8)
                    dve.wait_ge(gla_products, h * 9 + 7)
                    dve.wait_ge(gla_merged, h * 8 + 5)
                    tt(other[0][:, P:T], q[:, P:T], scaled[1][:, P:T], ALU.mult)
                    merge(5)
                    dve.wait_ge(gla_merged, h * 8 + 6)
                    signal(tt(k_dec[0][:, 0:3 * P], k[:, 0:3 * P], scaled[0][:, 0:3 * P], ALU.mult))
                    merge(6)
                    settle()
                    dve.wait_ge(gla_merged, h * 8 + 7)
                    dve.wait_ge(gla_products, h * 9 + 8)
                    ts(k_dec[1][:, P:2 * P], k_dec[0][:, P:2 * P], chunk_decay[:, 2:3], None, ALU.mult)
                    after(ts(k_dec[1][:, 0:P], k_dec[0][:, 0:P], chunk_decay[:, 1:2], None, ALU.mult))
                    ts(k_dec[1][:, 2 * P:3 * P], k_dec[1][:, 0:P], chunk_decay[:, 2:3], None, ALU.mult).then_inc(gla_factors, 1)
                    merge(7)
                    dve.wait_ge(head_squares, h + 1)
                    tt(square_sum[:, :], square_sum[:, :], gated, ALU.add).then_inc(head_summed, 1)
                    norm(h + norms[("gla", 0)], GDV, head_rstd)
                    for m in range(2):
                        row = rows(a_rows, h * 2 + (CAT + m))
                        after(stt(gated, ps[:, 4 + m, :], gla_gain[:, m:m + 1], head_rstd, ALU.mult, ALU.mult))
                        last = tt(row, row, gated, ALU.mult)
                        if m == 0:
                            after(last)
                    last.then_inc(head_gated, 1)

            def ssm_groups():
                dt_raw = small[DT0:DT0 + SH, :]
                after(ts(dt_rows, dt_raw, dt_bias, None, ALU.add))
                stt(far1, dt_rows, -1.0, dt_rows, ALU.mult, ALU.max).then_inc(dt_signal, 1)
                dve.wait_ge(dt_act, 1)
                ts(far2, far1, 1.0, None, ALU.add).then_inc(dt_signal, 1)
                dve.wait_ge(dt_act, 2)
                after(stt(far2, far2, 1.0, far1, ALU.subtract, ALU.subtract))
                after(tt(cum, cum, far2, ALU.subtract))
                after(stt(dt_rows, dt_rows, 0.0, cum, ALU.max, ALU.add))
                after(ts(cum, dt_rows, a_log, -1.0, ALU.mult, ALU.mult))
                for c in range(NC):
                    part = cum[:, c * P:c * P + P]
                    last = nc.vector.tensor_tensor_scan(part, ones[DT0:DT0 + SH, :], part, 0.0, ALU.mult, ALU.add)
                last.then_inc(dt_cum, 1)
                dve.wait_ge(dt_cum, 1)
                chunks = cum.rearrange("p (c t) -> p c t", c=NC)[:, 0:3, :]
                tt(far1[:, 0:3 * P].rearrange("p (c t) -> p c t", c=3), chunks[:, :, P - 1:P].to_broadcast([SH, 3, P]),
                   chunks, ALU.subtract).then_inc(dt_cum, 1)
                dve.wait_ge(dt_act, 3)
                ts(far2[:, P:2 * P], far1[:, P:2 * P], ssm_chunk_decay[:, 2:3], None, ALU.mult)
                after(ts(far2[:, 0:P], far1[:, 0:P], ssm_chunk_decay[:, 1:2], None, ALU.mult))
                ts(far2[:, 2 * P:3 * P], far2[:, 0:P], ssm_chunk_decay[:, 2:3], None, ALU.mult).then_inc(dt_far, 1)
                dve.wait_ge(cols_turned, 1)
                nc.vector.tensor_copy(ssm_cols[:, :, :].rearrange("p n h -> p (n h)"), ps[:, 4, 0:14 * SH]).then_inc(cols_ready, 1)
                dve.wait_ge(cols_ready, 1)
                diagonal_cb = diagonal(cb)
                with loop(SG, 5) as g:
                    heads = ds(g * 4, 4)

                    def head_row_of(r):
                        if r >= 2:
                            dve.wait_ge(row_spread, g * 4 + (r - 1))
                        ts(head_row[r % 2], cum, ident[DT0:DT0 + SH, ds(g * 4 + (DT0 + r), 1)], None, ALU.mult).then_inc(head_row_ready, 1)

                    def difference(r):
                        dve.wait_ge(from_start_ready, g * 4 + (r + 1))
                        if r >= 2:
                            dve.wait_ge(y_diag_done, g * 4 + (r - 1))
                        for c in range(NC):
                            last = ts(decay[r % 2][:, c * P:c * P + P], ps[:, r % 2, c * P:c * P + P],
                                      ssm_cols[:, 4 + c, ds(g * 4 + r, 1)], 0.0, ALU.subtract, ALU.min)
                        last.then_inc(decay_diff, 1)

                    def with_cb(r):
                        dve.wait_ge(decay_exp, g * 4 + (r + 1))
                        blocks = decay[r % 2].rearrange("p (c t) -> p c t", c=NC)
                        tt(blocks, blocks, diagonal_cb, ALU.mult).then_inc(decay_ready, 1)

                    head_row_of(0)
                    head_row_of(1)
                    dve.wait_ge(x_turned, g + 1)
                    for half in range(2):
                        dt_cols = ssm_cols[:, 2 * half:2 * half + 2, heads].unsqueeze(3).to_broadcast([P, 2, 4, 64])
                        last = tt(x_group[:, 2 * half:2 * half + 2, :].rearrange("p c (h v) -> p c h v", h=4),
                                  ps[:, half, :].rearrange("p (c h v) -> p c h v", c=2, h=4), dt_cols, ALU.mult)
                    last.then_inc(x_taken, 1)
                    dve.wait_ge(x_taken, g + 1)
                    dve.wait_ge(cb_far_taken, g + 1)
                    for jc in range(NC):
                        last = tt(cb[:, jc, jc, :], ps[:, 2 + jc, jc * P:jc * P + P], tri, ALU.mult)
                    after(last)
                    difference(0)
                    difference(1)
                    with_cb(0)
                    for n, (jc, ic) in enumerate(FAR):
                        cols = ssm_cols[:, 8 + n, heads].unsqueeze(2).to_broadcast([P, 4, 64])
                        last = tt(x_far[:, n, :].rearrange("p (h v) -> p h v", h=4), x_group[:, jc, :].rearrange("p (h v) -> p h v", h=4),
                                  cols, ALU.mult)
                    last.then_inc(x_far_ready, 1)
                    head_row_of(2)
                    with_cb(1)
                    difference(2)
                    head_row_of(3)
                    difference(3)
                    with_cb(2)
                    with_cb(3)
                    for m in range(2):
                        row = rows(a_rows, g * 2 + (CAT + 8 + m))
                        y_sum = (gated, rows(a_rows, 39))[m]
                        dve.wait_ge(y_far_done, g + 1)
                        dve.wait_ge(y_diag_done, g * 4 + (2 * m + 2))
                        dve.wait_ge(from_start_ready, g * 4 + (2 * m + 2))
                        tt(other[1][:, P:T], ps[:, 4 + m, P:T], from_start[m][:, P:T], ALU.mult)
                        after(stt(y_sum, xs_group[:, m, :], mixer_cols[:, ds(g * 2 + (86 + m), 1)], ps[:, 2 + m, :], ALU.mult, ALU.add))
                        after(tt(y_sum[:, P:T], y_sum[:, P:T], other[1][:, P:T], ALU.add))
                        tt(row, row, y_sum, ALU.mult).then_inc(y_gated, 1)
                    dve.wait_ge(group_squares, g + 1)
                    tt(square_sum[:, :], square_sum[:, :], other[0][:, :], ALU.add).then_inc(group_summed, 1)
                    norm(g + norms[("ssm", 0)], 256, head_rstd)
                    for m in range(2):
                        row = rows(a_rows, g * 2 + (CAT + 8 + m))
                        last = stt(row, row, mixer_cols[:, ds(g * 2 + (94 + m), 1)], head_rstd, ALU.mult, ALU.mult)
                    last.then_inc(group_done, 1)

            def odd():
                s = ODD
                slot = stages["latent"][0]
                for n in range(6):
                    dve.wait_ge(slot_done, slot + n + 1)
                    tt(rows(a_rows, LATENT + n), ps[:, (LATENT0 + n) % 4, :], rstd[:, :], ALU.mult).then_inc(tile_taken, 1)

                def latent_rows(start, count, name, number):
                    for m in range(1, count):
                        dve.wait_ge(latent_square, start + m + 1)
                        last = tt(square_sum[:, :], square_sum[:, :], other[m - 1][:, :], ALU.add)
                        if m < count - 1:
                            after(last)
                    last.then_inc(latent_summed, 1)
                    norm(norms[name], count * P)
                    for n in range(start, start + count):
                        stt(rows(a_rows, LATENT + n), rows(a_rows, LATENT + n), latent_gain[:, n:n + 1], rstd[:, :],
                            ALU.mult, ALU.mult).then_inc(latent_normed, 1)
                    for n in range(start, start + count):
                        dve.wait_ge(latent_hi_ready, n + 1)
                        tt(latent_lo[:, n, :], rows(a_rows, LATENT + n), latent_hi[:, n, :].bitcast(F32), ALU.subtract).then_inc(latent_lo_ready, 1)

                latent_rows(0, QR, "q_latent", 1)
                latent_rows(QR, KR, "kv_latent", 2)

                dve.wait_ge(odd_in, 48)
                after(nc.vector.tensor_copy(angle[1], angle[0].bitcast(I32)))
                after(ts(angle[0], angle[1], inv_freq, None, ALU.mult))
                for n, quarter in enumerate((0.0, 0.25)):
                    if n:
                        dve.wait_ge(table_ready, 1)
                    after(ts(angle[2], angle[0], 1.0 / (2.0 * np.pi), quarter, ALU.mult, ALU.add))
                    after(ts(angle[2], angle[2], ROUND, ROUND, ALU.add, ALU.subtract))
                    after(stt(angle[1], angle[2], -TURN[0], angle[0], ALU.mult, ALU.add))
                    after(stt(angle[1], angle[2], -TURN[1], angle[1], ALU.mult, ALU.add))
                    after(stt(angle[1], angle[2], -TURN[2], angle[1], ALU.mult, ALU.add))
                    after(ts(angle[1], angle[1], quarter * 2.0 * np.pi, PI_BELOW, ALU.add, ALU.min))
                    ts(angle[1], angle[1], -PI_BELOW, None, ALU.max).then_inc(angle_ready, 1)

                def rotate(j):
                    source = rows(a_rows, LATENT + 5 if j == 0 else QROPE + j - 1)
                    to = krope if j == 0 else source
                    dve.wait_ge(table_ready, 2)
                    dve.wait_ge(rope_turned, j + 1)
                    if j:
                        dve.wait_ge(rope_done, j)
                    tt(other[1][:, :], ps[:, 7, :], sin, ALU.mult).then_inc(rope_taken, 1)
                    after(tt(other[0][:, :], source, cos, ALU.mult))
                    tt(to, other[0][:, :], other[1][:, :], ALU.add).then_inc(rope_done, 1)

                slot = stages["k_up"][0]
                for i in range(2):
                    dve.wait_ge(slot_done, slot + i + 1)
                    for m in range(4):
                        nc.vector.tensor_copy(rows(a_rows, KN + 4 * i + m), ps[:, m, :]).then_inc(k_taken, 1)
                for j in range(1 + MH // 2):
                    rotate(j)

                with loop(MH // 2, 2 * 3) as i:
                    for e in range(2):
                        dve.wait_ge(scores_done, i * 8 + (4 * e + 4))
                        near = diagonal(ps[:, 0:NC, :].rearrange("p i (j t) -> p i j t", t=P))
                        after(tt(near, near, causal.unsqueeze(1).to_broadcast([P, NC, P]), ALU.add))
                        for qt in range(NC):
                            last = nc.vector.reduce_max(peak[:, qt:qt + 1], ps[:, qt, 0:(qt + 1) * P], AX_X)
                        after(last)
                        ts(peak_bias, peak, -SCORE_SCALE, None, ALU.mult).then_inc(bias_ready, 1)
                        dve.wait_ge(exp_done, i * 8 + (4 * e + 4))
                        after(nc.vector.reciprocal(prob_sum, prob_sum))
                        for qt in range(NC):
                            last = ts(probs[:, qt, 0:(qt + 1) * P], probs[:, qt, 0:(qt + 1) * P], prob_sum[:, qt:qt + 1], None, ALU.mult)
                        last.then_inc(probs_ready, 1)
                        for kc in (0, 2):
                            dve.wait_ge(probs_turned, i * 8 + (4 * e + kc + 1))
                            nc.vector.tensor_copy(probs_t[:, kc, kc * P:T], ps[:, 4 + kc % 2, kc * P:T]).then_inc(turned_dve, 1)
                        dve.wait_ge(o_hi_ready, i * 2 + (e + 1))
                        tt(rows_r(o_lo, i * 2 + e), ps[:, 6 + e, :], rows_r(o_hi, i * 2 + e).bitcast(F32), ALU.subtract).then_inc(o_lo_ready, 1)
                post_norm(s)

            dve.wait_ge(consts_in, 48)
            dve.wait_ge(x_in, 16)
            for s in range(N_SUB):
                if s not in (EVEN, ODD):
                    last = ts(post_gain(s), post_gain(s), 0.5, None, ALU.mult)
            last.then_inc(gains_halved, 1)
            for s in range(N_SUB):
                pre_norm(s)
                if s == EVEN:
                    even()
                elif s == ODD:
                    odd()
                else:
                    ffn(FFN_OF[s], s)
            for k in range(DK):
                add_update(N_SUB - 1, k)


def blocks_of(w):
    k, n = w.shape
    return w.reshape(k // P, P, n // P, P).transpose(2, 1, 0, 3).reshape(n // P, P, k)


def halves_of(blocks):
    n, _, k = blocks.shape
    return blocks.reshape(n, P, 2, k // 2).transpose(0, 2, 1, 3).reshape(2 * n, P, k // 2)


def merged(blocks, count):
    n, _, k = blocks.shape
    return blocks.reshape(n // count, count, P, k).transpose(0, 2, 1, 3).reshape(n // count, P, count * k)


def moving_of(w, per_slot):
    k, n = w.shape
    return (w.reshape(k // P // per_slot, per_slot, P, n // T, T).transpose(3, 0, 2, 1, 4)
            .reshape(-1, P, per_slot * T))


def columns_of(v):
    return v.reshape(-1, P).T


def constants():
    j, i = np.arange(P)[:, None], np.arange(P)[None, :]
    levels = [(j // (2 * n) == i // (2 * n)) & (j // n % 2 == 0) & (i // n % 2 == 1) for n in SPANS] + [j == i]
    turn = np.where(j % ROPE == i % ROPE + ROPE // 2, -1.0, 0.0) + np.where(j % ROPE + ROPE // 2 == i % ROPE, 1.0, 0.0)
    frequencies = (10000.0 ** (-np.arange(0, ROPE, 2, dtype=np.float32) / ROPE)).astype(np.float32)
    return {
        "ident": np.eye(P, dtype=np.float32),
        "level_mask": np.stack(levels, axis=1).astype(np.float32).reshape(P, -1),
        "tri": (j <= i).astype(np.float32),
        "causal": np.where(i <= j, 0.0, -1e30).astype(np.float32),
        "turn": (turn * (j // ROPE == i // ROPE)).astype(np.float32),
    }, np.tile(frequencies, 4)


def lay_out(a):
    arrays, frequencies = constants()
    names = [[f"{part}_{when}_norm" for part in ("ffn1", "mix", "ffn2")] for when in ("pre", "post")]
    arrays["gains"] = np.concatenate([columns_of(a[n][layer]) for group in names for layer in range(2) for n in group], axis=1)
    arrays["x_t"] = a["x"][0].T
    arrays["positions"] = a["positions"]
    for f in range(N_FFN):
        ffn, layer = ("ffn1", "ffn2")[f % 2], f // 2
        gate, up = blocks_of(a[ffn + "_w_gate"][layer]), blocks_of(a[ffn + "_w_up"][layer])
        arrays[f"w_gate_up{f}"] = np.stack([gate, up], axis=1).reshape(2 * FT, P, D)
        arrays[f"w_down{f}"] = halves_of(blocks_of(a[ffn + "_w_down"][layer]))

    w_in = a["ab_w_in"][0]
    sizes = (GH * P, GH * P, GH * GDV, GH * GDV, RANK, SH * SP_, SH * SP_ + 2 * SG * P, SH)
    q, k, v, g, a_low, z, xbc, dt = np.split(w_in, np.cumsum(sizes)[:-1], axis=1)
    small = np.zeros((D, P), np.float32)
    small[:, 0:RANK] = a_low
    small[:, DT0:DT0 + SH] = dt
    arrays["w_qk_small"] = blocks_of(np.concatenate([q, k, small], axis=1))
    arrays["w_v"] = moving_of(v, 2)
    arrays["w_g"], arrays["w_z"], arrays["w_xbc"] = blocks_of(g), blocks_of(z), blocks_of(xbc)
    arrays["w_even_out"] = halves_of(blocks_of(a["ab_w_out"][0]))
    arrays["gate2"] = a["gla_w_gate2"][0]

    down = a["mla_w_down"][0]
    arrays["w_latent"] = blocks_of(np.concatenate([down, down[:, (QR + KR) * P:]], axis=1))
    uq = a["mla_w_uq"][0].reshape(QR * P, MH, P + ROPE)
    pairs = [np.concatenate([uq[:, 2 * i, :P], uq[:, 2 * i + 1, :P], uq[:, 2 * i, P:], uq[:, 2 * i + 1, P:]], axis=1) for i in range(MH // 2)]
    arrays["w_q_up"] = merged(blocks_of(np.concatenate(pairs, axis=1)), 3)
    ukv = a["mla_w_ukv"][0].reshape(KR * P, MH, 2 * P)
    arrays["w_k_up"] = merged(blocks_of(ukv[:, :, :P].reshape(KR * P, MH * P)), 4)
    arrays["w_v_up"] = moving_of(ukv[:, :, P:].reshape(KR * P, MH * P), 2)
    arrays["w_odd_out"] = blocks_of(a["mla_w_o"][0])

    cols = np.zeros((P, 110), np.float32)
    cols[:, 0:64] = a["ssm_conv_w"][0].reshape(4, 16, P).transpose(2, 1, 0).reshape(P, 64)
    cols[:, 64:80] = columns_of(a["ssm_conv_b"][0])
    cols[:, 80:84] = columns_of(a["gla_b_gate2"][0])
    cols[:, 84:86] = columns_of(a["gla_norm"][0])
    cols[:, 86:94] = np.repeat(a["ssm_d"][0], SP_).reshape(8, P).T
    cols[:, 94:102] = columns_of(a["ssm_norm"][0])
    cols[DT0:DT0 + SH, 102] = a["ssm_dt_bias"][0]
    cols[DT0:DT0 + SH, 103] = a["ssm_a_log"][0]
    cols[:, 104:107] = columns_of(a["mla_q_norm"][0])
    cols[:, 107:109] = columns_of(a["mla_kv_norm"][0])
    cols[:, 109] = frequencies
    arrays["mixer_cols"] = cols
    return {k: np.ascontiguousarray(v) for k, v in arrays.items()}


def kernel(**inputs):
    import concourse.bacc as bacc
    from concourse.bass_utils import run_bass_kernel_spmd

    arrays = lay_out({k: np.asarray(v) for k, v in inputs.items()})
    nc = bacc.Bacc("TRN2", target_bir_lowering=False, num_devices=1)
    dram = {k: nc.dram_tensor("in_" + k, v.shape, mybir.dt.from_np(v.dtype), kind="ExternalInput").ap() for k, v in arrays.items()}
    out = nc.dram_tensor("out_t", (D, T), F32, kind="ExternalOutput").ap()
    build_trunk(nc, dram, out)
    result = run_bass_kernel_spmd(nc, [{"in_" + k: v for k, v in arrays.items()}], core_ids=[0])
    return result.results[0]["out_t"].T[None]
```

```python
from contextlib import ExitStack, contextmanager

import numpy as np

import concourse.bass as bass
from concourse import mybir

F32 = mybir.dt.float32
F32R = mybir.dt.float32r
I32 = mybir.dt.int32
U8 = mybir.dt.uint8
ALU = mybir.AluOpType
ACT = mybir.ActivationFunctionType
AX_X = mybir.AxisListType.X
ds = bass.ds

P = 128
T = 512
NC = T // P
D = 1024
DK = D // P
F = 2816
FT = F // P
EPS = 1e-6
N_FFN = 4
N_SUB = 6
EVEN, ODD = 1, 4

GH, GDV = 4, 256
RANK = 16
SPANS = (64, 32, 16, 8, 4, 2, 1)
SH, SV, SG = 16, 64, 4
DT0 = 32
MH, QR, KR, ROPE = 8, 3, 2, 64

RAW = 2
RING = 4
HALF = FT // 2
WIDTH = HALF * P
FFN_OF = {0: 0, 2: 1, 3: 2, 5: 3}
SCORE_SCALE = (P + ROPE) ** -0.5

ROUND = 1.5 * 2 ** 23
TURN_1 = 6.28125
TURN_2 = float(np.float32(round((2 * np.pi - TURN_1) * 2 ** 20) / 2 ** 20))
TURN = (TURN_1, TURN_2, 2 * np.pi - TURN_1 - TURN_2)
PI_BELOW = float(np.nextafter(np.float32(np.pi), np.float32(0)))


def plan_stages():
    ffn = [[(f"gate_up{f}", 2 * FT, DK * P), (f"down{f}", 2 * DK, WIDTH)] for f in range(N_FFN)]
    even = [("qk_small", 2 * GH + 1, D), ("v", 8, D), ("xbc", 16, D), ("zg", 16, D), ("even_out", 16, D)]
    odd = [("latent", 6, D), ("q_up", 4, 9 * P), ("k_up", 2, D), ("v_up", 2, D), ("odd_out", 8, D)]
    stages, first = {}, 0
    for name, slots, width in ffn[0] + even + ffn[1] + ffn[2] + odd + ffn[3]:
        stages[name] = (first, slots, width)
        first += slots
    return stages, first


def plan_norms():
    names = []
    for s in range(N_SUB):
        names.append((s, "pre"))
        if s == EVEN:
            names += [("gla", h) for h in range(GH)] + [("ssm", g) for g in range(SG)]
        if s == ODD:
            names += ["q_latent", "kv_latent"]
        names.append((s, "post"))
    return {name: n for n, name in enumerate(names)}


def build_trunk(nc, dram, out):
    stages, total_slots = plan_stages()
    norms = plan_norms()

    def width_of(slot):
        for first, slots, width in stages.values():
            if first <= slot < first + slots:
                return width

    with ExitStack() as ctx:
        def sb(name, shape, dt=F32):
            return ctx.enter_context(nc.sbuf_tensor(name, shape, dt))

        def sem(name):
            return ctx.enter_context(nc.semaphore(name))

        x = sb("x", [P, DK, T])
        raw = [sb(f"raw{r}", [P, WIDTH]) for r in range(RAW)]
        with ExitStack() as inner:
            ring_rows = inner.enter_context(nc.sbuf_tensor("ring_rows", [P, 2 * RING, WIDTH], F32))
        w_hi = [sb(f"w_hi{r}", [P, WIDTH], F32R) for r in range(RING)]
        w_lo = [sb(f"w_lo{r}", [P, WIDTH], F32R) for r in range(RING)]
        scaled = [sb(f"scaled{b}", [P, T]) for b in range(2)]
        other = [sb(f"other{b}", [P, T]) for b in range(2)]
        square = other
        diag = other[1][:, :].rearrange("p (c t) -> p c t", c=NC)
        rstd = sb("rstd", [P, T])
        square_sum = sb("square_sum", [P, T])
        ident = sb("ident", [P, P])
        ones = sb("ones", [P, P])
        gains = sb("gains", [P, 2 * N_SUB * DK])
        mixer_cols = sb("mixer_cols", [P, 132])
        mean = sb("mean", [P, NC])
        rstd_col = sb("rstd_col", [P, NC])
        minus_half = sb("minus_half", [P, NC])

        def pre_gain(s):
            return gains[:, DK * s:DK * s + DK]

        def post_gain(s):
            return gains[:, DK * (N_SUB + s):DK * (N_SUB + s) + DK]

        conv_w = mixer_cols[:, 0:64].rearrange("p (i k) -> p i k", k=4)
        conv_b = mixer_cols[:, 64:80]
        gla_bias = mixer_cols[:, 80:84]
        gla_gain = mixer_cols[:, 84:86]
        skip_col = mixer_cols[:, 86:94]
        ssm_gain = mixer_cols[:, 94:102]
        dt_bias = mixer_cols[DT0:DT0 + SH, 102:103]
        a_log = mixer_cols[DT0:DT0 + SH, 103:104]
        latent_gain = mixer_cols[:, 104:109]
        inv_freq = mixer_cols[:, 109:110]


        HROWS, AROWS = 2 * DK, 2 * FT

        def parts(*shapes):
            with ExitStack() as inner:
                return [inner.enter_context(nc.sbuf_tensor(name, [P, rows, T], dt)) for name, rows, dt in shapes]

        o_hi, o_lo = parts(("o_hi", MH, F32R), ("o_lo", MH, F32R))
        cat_lo, = parts(("cat_lo", 16, F32R))
        h_rows, = parts(("h_rows", HROWS, F32))
        h_hi = sb("h_hi", [P, DK, T], F32R)
        h_lo = sb("h_lo", [P, DK, T], F32R)

        _, cat_hi = parts(("before_cat_hi", 24, F32), ("cat_hi", 16, F32R))
        _, latent_hi, latent_lo = parts(("before_latent", 32, F32), ("latent_hi", 5, F32R), ("latent_lo", 5, F32R))
        a_rows, = parts(("a_rows", AROWS, F32))
        a_hi = sb("a_hi", [P, FT, T], F32R)
        a_lo = sb("a_lo", [P, FT, T], F32R)

        def rows(region, at, count=1):
            if isinstance(at, int):
                return region[:, at:at + count, :].rearrange("p r t -> p (r t)")
            return region[:, :, :].rearrange("p r t -> p (r t)")[:, ds(at * T, count * T)]

        def rows_r(tensor, at):
            return rows(tensor, at)

        spare = [ring_rows[:, n, D:WIDTH] for n in range(2 * RING)] + [r[:, D:WIDTH] for r in raw]

        XS, B_ROWS, C_ROWS, Q, K, V = 0, 8, 12, 16, 20, 24
        CAT = [Q + h + m * GH for m in range(2) for h in range(GH)] + [XS + k for k in range(8)]
        small = rows(a_rows, 32)
        HALF_P = P // 2
        MASKS = len(SPANS) * HALF_P + P
        level_mask = rows(a_rows, 34)[:, 0:MASKS // 4].bitcast(U8)
        tri = rows(a_rows, 34)[:, 256:384]
        gate2 = rows(a_rows, 35)[0:RANK, :]
        LOG_A = 37
        head_rstd = rows(a_rows, 43)
        dt_rows, cum, far1, far2 = [rows(a_rows, n)[DT0:DT0 + SH, :] for n in (33, 32, 42, 43)]
        ssm_cols = spare[8][:, 0:14 * SH].rearrange("p (n h) -> p n h", h=SH)
        scores = rows(a_rows, 33).rearrange("p (c t) -> p c t", c=NC)
        far_blocks = [spare[4], spare[5][:, 0:2 * P], spare[5][:, 2 * P:3 * P]]
        k_dec = [rows(a_rows, 35 + b) for b in range(2)]
        conv_in = [rows(a_rows, 41 + b) for b in range(2)]
        v_head = [spare[c][:, 0:GDV] for c in range(NC)]
        cb = scores
        x_group = [spare[c][:, 0:4 * SV] for c in range(NC)]
        x_far = rows(a_rows, 24, 3).rearrange("p (n v) -> p n v", n=6)
        decay = [rows(a_rows, 27 + b) for b in range(2)]
        from_start = [rows(a_rows, 29 + b) for b in range(2)]
        b_group = rows(a_rows, 31)
        xs_group = rows(a_rows, 35, 2).rearrange("p (m t) -> p m t", m=2)
        y_sum = [rows(a_rows, row) for row in (37, 39)]
        head_row = [rows(a_rows, 41 + b)[DT0:DT0 + SH, :] for b in range(2)]

        QN, QROPE, KN, VT, LATENT = 0, 8, 12, 20, 20
        cos, sin, krope = rows(a_rows, 28), rows(a_rows, 29), rows(a_rows, 30)
        causal, turn_mat = rows(a_rows, 31)[:, 0:P], rows(a_rows, 31)[:, P:2 * P]
        probs = rows(a_rows, 32, 4).rearrange("p (i k) -> p i k", i=NC)
        probs_t = rows(a_rows, 36, 4).rearrange("p (j q) -> p j q", j=NC)
        q_head, q_pair = rows(a_rows, 40), rows(a_rows, 41)
        v_pair = rows(a_rows, 42, 2).rearrange("p (c v) -> p c v", c=NC)
        angle = [rows(a_rows, row) for row in (42, 43, 30)]
        peak = mixer_cols[:, 112:116]
        peak_bias = mixer_cols[:, 116:120]
        prob_sum = mixer_cols[:, 120:124]
        chunk_decay = mixer_cols[:, 124:128]
        ssm_chunk_decay = mixer_cols[DT0:DT0 + SH, 128:132]

        def u_row(s, k):
            return rows(a_rows, {EVEN: XS, ODD: VT}[s] + k) if s in (EVEN, ODD) else rows(h_rows, k)

        ps = ctx.enter_context(nc.psum_tensor("ps", [P, 8, T], F32))
        NORM = 7
        SPLITS_BEFORE_NORM = {"xbc": 3, "zg": 2}
        XBC_BANKS, ZG_BANKS = (2, 3), (1, 6)
        QK0, V0, XBC0, ZG0, LATENT0 = 0, 9, 17, 33, 49

        consts_in, gains_in, even_in, odd_in = sem("consts_in"), sem("gains_in"), sem("even_in"), sem("odd_in")
        x_in = [sem(f"x_in{k}") for k in range(DK)]
        consts_made, gains_halved = sem("consts_made"), sem("gains_halved")
        raw_in = [sem(f"raw_in{r}") for r in range(RAW)]
        early_in = [sem(f"early_in{r}") for r in range(RAW)]
        hi_done, lo_done = sem("hi_done"), sem("lo_done")
        slot_done = sem("slot_done")
        residual_ready, h_hi_ready, h_lo_ready = sem("residual_ready"), sem("h_hi_ready"), sem("h_lo_ready")
        pre_square, pre_summed = sem("pre_square"), sem("pre_summed")
        post_square, post_summed, u_ready = sem("post_square"), sem("post_summed"), sem("u_ready")
        sums_ready, mean_ready, rstd_col_ready = sem("sums_ready"), sem("mean_ready"), sem("rstd_col_ready")
        diag_ready, spread_ready, rstd_ready = sem("diag_ready"), sem("spread_ready"), sem("rstd_ready")
        gate_scaled, up_scaled, silu_done = sem("gate_scaled"), sem("up_scaled"), sem("silu_done")
        a_ready, a_hi_ready, a_lo_ready = sem("a_ready"), sem("a_hi_ready"), sem("a_lo_ready")
        dve_step, act_step, stored = sem("dve_step"), sem("act_step"), sem("stored")
        tile_taken, row_silu = sem("tile_taken"), sem("row_silu")
        conv_started, conv_step, conv_done = sem("conv_started"), sem("conv_step"), sem("conv_done")
        decay_logits, logit_ready, softplus_ready = sem("decay_logits"), sem("logit_ready"), sem("softplus_ready")
        log_a_ready = sem("log_a_ready")
        gla_diff, gla_decay, gla_factors = sem("gla_diff"), sem("gla_decay"), sem("gla_factors")
        gla_products, gla_merged, far_taken = sem("gla_products"), sem("gla_merged"), sem("far_taken")
        key_copied, value_copied, gla_out = sem("key_copied"), sem("value_copied"), sem("gla_out")
        head_squares, head_summed = sem("head_squares"), sem("head_summed")
        dt_signal, dt_act, dt_cum, dt_far = sem("dt_signal"), sem("dt_act"), sem("dt_cum"), sem("dt_far")
        cols_turned, cols_ready = sem("cols_turned"), sem("cols_ready")
        group_copied, x_turned, x_taken, x_far_ready = sem("group_copied"), sem("x_turned"), sem("x_taken"), sem("x_far_ready")
        cb_ready, cb_taken, cb_far_taken = sem("cb_ready"), sem("cb_taken"), sem("cb_far_taken")
        head_row_ready, row_spread, from_start_ready = sem("head_row_ready"), sem("row_spread"), sem("from_start_ready")
        decay_diff, decay_exp, decay_ready = sem("decay_diff"), sem("decay_exp"), sem("decay_ready")
        y_diag_done, y_far_done, y_gated = sem("y_diag_done"), sem("y_far_done"), sem("y_gated")
        group_squares, group_summed, group_done = sem("group_squares"), sem("group_summed"), sem("group_done")
        cat_hi_ready, cat_lo_ready = sem("cat_hi_ready"), sem("cat_lo_ready")
        angle_ready, table_ready = sem("angle_ready"), sem("table_ready")
        latent_square, latent_summed, latent_normed = sem("latent_square"), sem("latent_summed"), sem("latent_normed")
        latent_hi_ready, latent_lo_ready = sem("latent_hi_ready"), sem("latent_lo_ready")
        q_taken, k_taken, v_taken = sem("q_taken"), sem("k_taken"), sem("v_taken")
        rope_turned, rope_taken, rope_done = sem("rope_turned"), sem("rope_taken"), sem("rope_done")
        pair_copied, q_copied, scores_done, bias_ready = sem("pair_copied"), sem("q_copied"), sem("scores_done"), sem("bias_ready")
        exp_done, probs_ready, probs_turned = sem("exp_done"), sem("probs_ready"), sem("probs_turned")
        turned_act, att_done = sem("turned_act"), sem("att_done")
        o_hi_ready, o_lo_ready = sem("o_hi_ready"), sem("o_lo_ready")

        block = ctx.enter_context(nc.Block())

        def raw_of(slot, width):
            if RAW <= slot < 2 * RAW:
                return rows(a_rows, 2 * (slot - RAW), 2)[:, 0:width]
            return raw[slot % RAW][:, 0:width]

        def diagonal(blocks):
            first = blocks[:, :, 0, :]
            (part, row, col) = first.ap
            return bass.AP(tensor=first.tensor, offset=first.offset, ap=[list(part), [row[0] + P, NC], list(col)])

        ROW_BANKS = (0, 5)
        CB_AT = ((2, 0), (3, P), (5, 0), (5, 2 * P))
        FAR = [(0, 1), (1, 2), (2, 3), (0, 2), (1, 3), (0, 3)]

        @block.sync
        def _(sp):

            def load_slot(src, index, slot, turns, width):
                if slot >= RAW or not isinstance(turns, int):
                    sp.wait_ge(lo_done, slot - 1 + turns)
                sp.dma_start(raw[slot % RAW][:, 0:width], src[index]).then_inc(raw_in[slot % RAW], 16)

            for n in range(RAW):
                load_slot(dram["w_gate_up0"], n, n, 0, width_of(n))
            x_rows = dram["x_t"].rearrange("(k p) t -> p k t", p=P)
            for k in range(DK):
                sp.dma_start(x[:, k, :], x_rows[:, k, :]).then_inc(x_in[k], 16)
                if k < RAW:
                    sp.dma_start(raw_of(RAW + k, D), dram["w_gate_up0"][RAW + k]).then_inc(early_in[k], 16)
            for name, (first, slots, width) in stages.items():
                src = dram["w_" + name]
                turns = slots // 4
                if turns > 1 and first >= RAW:
                    with sp.Fori(0, turns) as turn:
                        for n in range(4):
                            load_slot(src, turn * 4 + n, first + n, turn * 4, width)
                    for n in range(4 * turns, slots):
                        load_slot(src, n, first + n, 0, width)
                    continue
                for n in range(2 * RAW if first == 0 else 0, min(slots, 4)):
                    load_slot(src, n, first + n, 0, width)
                if turns > 1:
                    with sp.Fori(1, turns) as turn:
                        for n in range(4):
                            load_slot(src, turn * 4 + n, first + n, turn * 4, width)
                for n in range(max(4, 4 * turns), slots):
                    load_slot(src, n, first + n, 0, width)
            out_rows = out.rearrange("(k p) t -> p k t", p=P)
            for k in range(DK):
                sp.wait_ge(residual_ready, DK * (N_SUB - 1) + k + 1)
                sp.dma_start(out_rows[:, k, :], x[:, k, :]).then_inc(stored, 16)
            sp.wait_ge(stored, 16 * DK)

        @block.gpsimd
        def _(pool):
            nc.gpsimd.memset(ones[:, :], 1.0).then_inc(consts_made, 1)
            nc.gpsimd.memset(minus_half[:, :], -0.5).then_inc(consts_made, 1)
            pool.wait_ge(consts_made, 2)

            def split_low(slot, turns, width):
                pool.wait_ge(hi_done, slot + 1 + turns)
                if slot >= RING:
                    pool.wait_ge(slot_done, slot - RING + 1 + turns)
                nc.gpsimd.tensor_tensor(w_lo[slot % RING][:, 0:width], raw_of(slot, width),
                                        w_hi[slot % RING][:, 0:width].bitcast(F32), ALU.subtract).then_inc(lo_done, 1)

            def split_stage(name, done=0):
                first, slots, width = stages[name]
                turns = (slots - done) // 4
                if turns:
                    with pool.Fori(0, turns) as turn:
                        for n in range(4):
                            split_low(first + done + n, turn * 4, width)
                for n in range(done + 4 * turns, slots):
                    split_low(first + n, 0, width)

            def split_some(name, start, stop):
                first = stages[name][0]
                for n in range(start, stop):
                    split_low(first + n, 0, width_of(first + n))

            def power(n):
                pool.wait_ge(mean_ready, n + 1)
                nc.gpsimd.tensor_tensor(rstd_col[:, :], mean[:, :], minus_half[:, :], ALU.pow).then_inc(rstd_col_ready, 1)

            def pre_sum(s):
                for k in range(1, DK):
                    pool.wait_ge(pre_square, DK * s + k + 1)
                    if k > 1:
                        pool.wait_ge(pre_summed, (DK - 1) * s + k - 1)
                    nc.gpsimd.tensor_tensor(square_sum[:, :], square_sum[:, :], square[k % 2][:, :], ALU.add).then_inc(pre_summed, 1)
                power(norms[(s, "pre")])

            first_stage = ["gate_up0", "qk_small", "gate_up1", "gate_up2", "latent", "gate_up3"]
            last_stage = ["down0", "even_out", "down1", "down2", "odd_out", "down3"]
            split_some("gate_up0", 0, 2)
            for s in range(N_SUB):
                split_some(first_stage[s], 2, RING)
                pre_sum(s)
                split_stage(first_stage[s], RING)
                if s == EVEN:
                    split_stage("v")
                    split_some("xbc", 0, RING)
                    for name, count, norm in (("xbc", GH, ("gla", 0)), ("zg", SG, ("ssm", 0))):
                        with pool.Fori(0, count) as turn:
                            for n in range(4):
                                if n == SPLITS_BEFORE_NORM[name]:
                                    power(turn + norms[norm])
                                split_low(stages[name][0] + RING + n, turn * 4, D)
                    split_stage("even_out", RING)
                elif s == ODD:
                    split_some("q_up", 0, 2)
                    power(norms["q_latent"])
                    split_some("q_up", 2, 4)
                    power(norms["kv_latent"])
                    split_stage("k_up")
                    split_stage("v_up")
                    split_stage("odd_out")
                else:
                    split_stage(last_stage[s])
                if s + 1 < N_SUB:
                    split_some(first_stage[s + 1], 0, 2)
                power(norms[(s, "post")])

        @block.scalar
        def _(act):
            steps = [0]

            def after(ins, turns=0, per_turn=0):
                steps[0] += 1
                ins.then_inc(act_step, 1)
                act.wait_ge(act_step, turns * per_turn + steps[0] if per_turn else steps[0])

            def copy(to, source, scale=1.0):
                return nc.scalar.activation(to, source, ACT.Copy, scale=scale)

            def split_high(slot, turns, width):
                if RAW <= slot < 2 * RAW:
                    act.wait_ge(early_in[slot - RAW], 16)
                else:
                    act.wait_ge(raw_in[slot % RAW], 16 * max(1, slot // RAW) + turns * 8)
                if slot >= RING:
                    act.wait_ge(slot_done, slot - RING + 1 + turns)
                    act.wait_ge(lo_done, slot - RING + 1 + turns)
                copy(w_hi[slot % RING][:, 0:width], raw_of(slot, width)).then_inc(hi_done, 1)

            def split_then(name, per_tile, take):
                first, slots, width = stages[name]
                per_turn, tiles = 4 // per_tile, slots // per_tile
                turns = max(0, slots - RING) // 4
                if turns > 1:
                    with act.Fori(0, turns) as turn:
                        for n in range(per_turn):
                            for m in range(per_tile):
                                split_high(first + RING + n * per_tile + m, turn * 4, width)
                            take(turn * per_turn + n, n)
                else:
                    turns = 0
                for tile in range(turns * per_turn, tiles):
                    last = tile == tiles - 1
                    if last:
                        take(tile, tile % per_turn)
                    for m in range(per_tile):
                        slot = first + RING + tile * per_tile + m
                        if slot < total_slots:
                            split_high(slot, 0, width_of(slot))
                    if not last:
                        take(tile, tile % per_turn)

            def pre_norm(s):
                for k in range(DK):
                    if s:
                        act.wait_ge(residual_ready, DK * (s - 1) + k + 1)
                    else:
                        act.wait_ge(x_in[k], 16)
                        if k in (1, 2):
                            split_high(RAW + k - 1, 0, width_of(RAW + k - 1))
                    copy(h_hi[:, k, :], x[:, k, :], pre_gain(s)[:, k:k + 1]).then_inc(h_hi_ready, 1)
                    if k >= 3:
                        act.wait_ge(pre_summed, (DK - 1) * s + k - 2)
                    nc.scalar.activation(square_sum[:, :] if k == 0 else square[k % 2][:, :], x[:, k, :],
                                         ACT.Square).then_inc(pre_square, 1)

            def take_out(s, name, per_tile):
                region, base = {EVEN: (a_rows, XS), ODD: (a_rows, VT)}.get(s, (h_rows, 0))

                def take(tile, n):
                    b = n % 2
                    act.wait_ge(slot_done, tile * per_tile + (stages[name][0] + per_tile))
                    square_first = isinstance(tile, int) and tile == DK - 1
                    if not square_first:
                        copy(rows(region, tile + base), ps[:, 4 + b, :], post_gain(s)[:, ds(tile, 1)]).then_inc(u_ready, 1)
                    act.wait_ge(post_summed, tile + (DK * s + 1))
                    nc.scalar.activation(square[b][:, :], ps[:, 4 + b, :], ACT.Square).then_inc(post_square, 1)
                    if square_first:
                        copy(rows(region, tile + base), ps[:, 4 + b, :], post_gain(s)[:, ds(tile, 1)]).then_inc(u_ready, 1)

                split_then(name, per_tile, take)

            def ffn(f, s):
                def take(tile, b):
                    act.wait_ge(gate_scaled, tile + (FT * f + 1))
                    nc.scalar.activation(scaled[b][:, :], scaled[b][:, :], ACT.Silu).then_inc(silu_done, 1)
                    act.wait_ge(a_ready, tile + (FT * f + 1))
                    copy(rows_r(a_hi, tile), scaled[b][:, :]).then_inc(a_hi_ready, 1)

                split_then(f"gate_up{f}", 2, take)
                take_out(s, f"down{f}", 2)

            def even():
                s = EVEN

                def softplus(tile, _):
                    if tile == 4:
                        for h in range(GH):
                            act.wait_ge(logit_ready, h + 1)
                            after(nc.scalar.activation(other[h % 2][:, :], other[h % 2][:, :], ACT.Exp, scale=-1.0))
                            nc.scalar.activation(other[h % 2][:, :], other[h % 2][:, :], ACT.Ln, bias=1.0).then_inc(softplus_ready, 1)

                def step_sizes(tile, _):
                    if tile == 0:
                        act.wait_ge(dt_signal, 1)
                        nc.scalar.activation(far1, far1, ACT.Exp, scale=-1.0)
                        nc.scalar.activation(a_log, a_log, ACT.Exp).then_inc(dt_act, 1)
                    if tile == 1:
                        act.wait_ge(dt_signal, 2)
                        nc.scalar.activation(cum, far2, ACT.Ln).then_inc(dt_act, 1)
                    if tile == 2:
                        act.wait_ge(dt_cum, 1)
                        nc.scalar.activation(ssm_chunk_decay, cum[:, P - 1:T:P], ACT.Exp)
                        act.wait_ge(dt_cum, 2)
                        nc.scalar.activation(far1[:, 0:3 * P], far1[:, 0:3 * P], ACT.Exp).then_inc(dt_act, 1)

                split_then("qk_small", 1, softplus)
                split_then("v", 1, step_sizes)
                gla_heads()
                ssm_groups()
                act.wait_ge(group_done, SG)
                for k in range(len(CAT)):
                    copy(cat_hi[:, k, :], rows(a_rows, CAT[k])).then_inc(cat_hi_ready, 1)
                take_out(s, "even_out", 2)

            def gla_heads():
                first = stages["xbc"][0] + RING
                act.wait_ge(log_a_ready, GH)
                with act.Fori(0, GH) as h:
                    log_a = rows(a_rows, h + LOG_A)

                    def conv_first(n):
                        act.wait_ge(tile_taken, h * 4 + (XBC0 + n + 1))
                        nc.scalar.activation(rows(a_rows, h * 4 + (XS + n)), conv_in[n % 2], ACT.Identity,
                                             bias=mixer_cols[:, ds(h * 4 + (64 + n), 1)],
                                             scale=mixer_cols[:, ds(h * 16 + (4 * n + 3), 1)]).then_inc(conv_started, 1)

                    def decay_of(j):
                        act.wait_ge(gla_diff, h * 8 + (j + 1))
                        nc.scalar.activation(scaled[j % 2][:, :], scaled[j % 2][:, :], ACT.Exp).then_inc(gla_decay, 1)

                    for c in range(NC):
                        last = copy(v_head[c], rows(a_rows, V + 2 * c, 2)[:, ds(h * GDV, GDV)])
                    last.then_inc(value_copied, 1)
                    for j in range(3):
                        decay_of(j)
                    conv_first(0)
                    decay_of(3)
                    split_high(first, h * 4, D)
                    for j in range(4, len(SPANS)):
                        decay_of(j)
                    act.wait_ge(gla_products, h * 9 + 6)
                    copy(k_dec[1], rows(a_rows, h + K)).then_inc(key_copied, 1)
                    act.wait_ge(gla_factors, h * 8 + 6)
                    nc.scalar.activation(scaled[1][:, P:T], log_a[:, P:T], ACT.Exp)
                    nc.scalar.activation(chunk_decay, log_a[:, P - 1:T:P], ACT.Exp)
                    act.wait_ge(gla_diff, h * 8 + 8)
                    nc.scalar.activation(scaled[0][:, 0:3 * P], scaled[0][:, 0:3 * P], ACT.Exp).then_inc(gla_decay, 1)
                    conv_first(1)
                    split_high(first + 1, h * 4, D)
                    act.wait_ge(gla_products, h * 9 + 9)
                    copy(far_blocks[0], ps[:, 4, 0:3 * P])
                    copy(spare[5], ps[:, 5, 0:3 * P]).then_inc(far_taken, 1)
                    conv_first(2)
                    split_high(first + 2, h * 4, D)
                    act.wait_ge(gla_out, h + 1)
                    nc.scalar.activation(square_sum[:, :], ps[:, 4, :], ACT.Square)
                    nc.scalar.activation(other[0][:, :], ps[:, 5, :], ACT.Square).then_inc(head_squares, 1)
                    split_high(first + 3, h * 4, D)

            def ssm_groups():
                first = stages["zg"][0] + RING
                act.wait_ge(conv_done, 4 * GH)
                with act.Fori(0, SG) as g:
                    def silu(n):
                        act.wait_ge(tile_taken, g * 4 + (ZG0 + n + 1))
                        nc.scalar.activation(scaled[n % 2][:, :], scaled[n % 2][:, :], ACT.Silu).then_inc(row_silu, 1)

                    def exponentials(r):
                        half = slice(64 * (r % 2), 64 * (r % 2) + 64)
                        act.wait_ge(row_spread, g * 4 + (r + 1))
                        nc.scalar.activation(from_start[r // 2][half, :], ps[half, ROW_BANKS[r % 2], :], ACT.Exp).then_inc(from_start_ready, 1)
                        act.wait_ge(decay_diff, g * 4 + (r + 1))
                        nc.scalar.activation(decay[r % 2], decay[r % 2], ACT.Exp).then_inc(decay_exp, 1)

                    nc.scalar.activation(rows(a_rows, 35, 2), rows(a_rows, g * 2 + XS, 2), ACT.Silu)
                    nc.scalar.activation(b_group, rows(a_rows, g + B_ROWS), ACT.Silu)
                    nc.scalar.activation(rows(a_rows, g + C_ROWS), rows(a_rows, g + C_ROWS), ACT.Silu).then_inc(group_copied, 1)
                    act.wait_ge(cb_ready, g + 1)
                    copy(far_blocks[0], ps[:, 2, P:T])
                    copy(far_blocks[1], ps[:, 3, 2 * P:T])
                    copy(far_blocks[2], ps[:, 5, P:2 * P]).then_inc(cb_far_taken, 1)
                    exponentials(0)
                    exponentials(1)
                    split_high(first, g * 4, D)
                    exponentials(2)
                    exponentials(3)
                    split_high(first + 1, g * 4, D)
                    silu(0)
                    act.wait_ge(y_gated, g * 2 + 1)
                    silu(1)
                    nc.scalar.activation(square_sum[:, :], rows(a_rows, g * 2 + XS), ACT.Square)
                    act.wait_ge(y_gated, g * 2 + 2)
                    silu(2)
                    nc.scalar.activation(other[0][:, :], rows(a_rows, g * 2 + (XS + 1)), ACT.Square).then_inc(group_squares, 1)
                    split_high(first + 2, g * 4, D)
                    silu(3)
                    split_high(first + 3, g * 4, D)

            def odd():
                s = ODD

                def square_q(tile, n):
                    if tile == 3:
                        act.wait_ge(tile_taken, LATENT0 + QR)
                        for n in range(QR):
                            nc.scalar.activation((square_sum, *other)[n][:, :], rows(a_rows, LATENT + n), ACT.Square).then_inc(latent_square, 1)

                split_then("latent", 1, square_q)
                for n in range(QR):
                    act.wait_ge(latent_normed, n + 1)
                    copy(latent_hi[:, n, :], rows(a_rows, LATENT + n)).then_inc(latent_hi_ready, 1)
                for n in range(KR):
                    nc.scalar.activation((square_sum, *other)[n][:, :], rows(a_rows, LATENT + QR + n), ACT.Square).then_inc(latent_square, 1)
                for n in range(QR, QR + KR):
                    act.wait_ge(latent_normed, n + 1)
                    copy(latent_hi[:, n, :], rows(a_rows, LATENT + n)).then_inc(latent_hi_ready, 1)

                def take_q(tile, n):
                    act.wait_ge(slot_done, stages["q_up"][0] + tile + 1)
                    for m, row in enumerate((QN + 2 * tile, QN + 2 * tile + 1, QROPE + tile)):
                        copy(rows(a_rows, row), ps[:, 3 * (tile % 2) + m, :]).then_inc(q_taken, 1)
                split_then("q_up", 1, take_q)
                for n in range(2):
                    act.wait_ge(angle_ready, n + 1)
                    nc.scalar.activation((sin, cos)[n], angle[1], ACT.Sin).then_inc(table_ready, 1)
                split_then("k_up", 1, lambda tile, n: None)

                def take_v(tile, n):
                    act.wait_ge(slot_done, stages["v_up"][0] + tile + 1)
                    act.wait_ge(rope_done, 1)
                    for c in range(NC):
                        copy(rows(a_rows, VT + 2 * c + tile), ps[:, c, :]).then_inc(v_taken, 1)
                split_then("v_up", 1, take_v)

                act.wait_ge(rope_done, 2)

                def copy_q(i, n):
                    if n % 2 == 0:
                        copy(q_pair, rows(a_rows, i + (QROPE + n // 2)))
                    copy(q_head, rows(a_rows, i * 2 + (QN + n))).then_inc(q_copied, 1)

                def copy_v(i):
                    copy(v_pair, rows(a_rows, VT, 8).rearrange("p (c v) -> p c v", c=NC)[:, :, ds(i * 256, 256)]).then_inc(pair_copied, 1)

                def exponentials(i, n):
                    act.wait_ge(bias_ready, i * 2 + (n + 1))
                    for qt in range(NC):
                        nc.scalar.activation(probs[:, qt, 0:(qt + 1) * P], ps[:, qt, 0:(qt + 1) * P], ACT.Exp,
                                             bias=peak_bias[:, qt:qt + 1], scale=SCORE_SCALE,
                                             accum_out=prob_sum[:, qt:qt + 1]).then_inc(exp_done, 1)

                def pair(i, last):
                    for n in range(2):
                        for kc in range(NC):
                            act.wait_ge(probs_turned, i * 8 + (4 * n + kc + 1))
                            copy(probs_t[:, kc, kc * P:T], ps[:, 4 + kc % 2, kc * P:T]).then_inc(turned_act, 1)
                        if not last:
                            act.wait_ge(scores_done, i * 8 + (4 * n + 8))
                            copy_q(i, n + 2)
                        if not last or n == 0:
                            exponentials(i, n + 1)
                        act.wait_ge(att_done, i * 2 + (n + 1))
                        copy(rows_r(o_hi, i * 2 + n), ps[:, 6 + n, :]).then_inc(o_hi_ready, 1)
                    if not last:
                        copy_v(i + 1)

                copy_q(0, 0)
                act.wait_ge(v_taken, 2 * NC)
                copy_v(0)
                act.wait_ge(rope_done, 1 + MH // 2)
                act.wait_ge(scores_done, 4)
                copy_q(0, 1)
                exponentials(0, 0)
                with act.Fori(0, MH // 2 - 1) as i:
                    pair(i, False)
                pair(MH // 2 - 1, True)
                take_out(s, "odd_out", 1)

            act.dma_start(gains[:, :], dram["gains"]).then_inc(gains_in, 16)
            act.dma_start(ident[:, :], dram["ident"]).then_inc(consts_in, 16)
            act.dma_start(mixer_cols[:, 0:110], dram["mixer_cols"]).then_inc(consts_in, 16)
            for n in range(RAW):
                split_high(n, 0, width_of(n))
            act.wait_ge(gains_halved, 1)
            for s in range(N_SUB):
                if s == EVEN:
                    act.dma_start(rows(a_rows, XS, 2)[:, 0:MASKS], dram["level_mask"]).then_inc(even_in, 16)
                    act.dma_start(tri, dram["tri"]).then_inc(even_in, 16)
                    act.dma_start(gate2, dram["gate2"]).then_inc(even_in, 16)
                if s == ODD:
                    act.dma_start(angle[0].bitcast(I32), dram["positions"].to_broadcast([P, T])).then_inc(odd_in, 16)
                    act.dma_start(causal, dram["causal"]).then_inc(odd_in, 16)
                    act.dma_start(turn_mat, dram["turn"]).then_inc(odd_in, 16)
                pre_norm(s)
                if s == EVEN:
                    even()
                elif s == ODD:
                    odd()
                else:
                    ffn(FFN_OF[s], s)

        @block.tensor
        def _(pe):
            def products(bank, slot, column, hi, lo, first, last):
                w_h = w_hi[slot % RING][:, column:column + P]
                w_l = w_lo[slot % RING][:, column:column + P]
                nc.tensor.matmul(ps[:, bank, :], w_h, hi, start=first, stop=False)
                nc.tensor.matmul(ps[:, bank, :], w_h, lo, start=False, stop=False)
                return nc.tensor.matmul(ps[:, bank, :], w_l, hi, start=False, stop=last)

            def slot_ready(slot, turns=0):
                pe.wait_ge(hi_done, slot + 1 + turns)
                pe.wait_ge(lo_done, slot + 1 + turns)

            def norm_sums(source_summed, count):
                pe.wait_ge(source_summed, count)
                for c in range(NC):
                    last = nc.tensor.matmul(ps[:, NORM, c:c + 1], square_sum[:, c * P:c * P + P], ones[:, 0:1], start=True, stop=True)
                last.then_inc(sums_ready, 1)

            def norm_spread(n):
                pe.wait_ge(diag_ready, n + 1)
                nc.tensor.matmul(ps[:, NORM, :], ones[:, :], other[1][:, :], start=True, stop=True).then_inc(spread_ready, 1)

            def first_four(s, name, bank0):
                first = stages[name][0]
                for m in range(2):
                    slot_ready(first + m)

                def behind(k):
                    for m in (2, 3):
                        if k == 0:
                            slot_ready(first + m)
                        last = products((bank0 + m) % 4, first + m, k * P, h_hi[:, k, :], h_lo[:, k, :], k == 0, k == DK - 1)
                        if k == DK - 1:
                            last.then_inc(slot_done, 1)

                for k in range(DK):
                    pe.wait_ge(h_hi_ready, DK * s + k + 1)
                    for m in range(2):
                        for w in (w_hi, w_lo):
                            nc.tensor.matmul(ps[:, (bank0 + m) % 4, :], w[(first + m) % RING][:, k * P:k * P + P], h_hi[:, k, :],
                                             start=k == 0 and w is w_hi, stop=False)
                    pe.wait_ge(h_lo_ready, DK * s + k + 1)
                    for m in range(2):
                        last = nc.tensor.matmul(ps[:, (bank0 + m) % 4, :], w_hi[(first + m) % RING][:, k * P:k * P + P], h_lo[:, k, :],
                                                start=False, stop=k == DK - 1)
                        if k == DK - 1:
                            last.then_inc(slot_done, 1)
                    if k % 2:
                        behind(k // 2)
                behind(4)
                norm_sums(pre_summed, (DK - 1) * (s + 1))
                behind(5)
                behind(6)
                norm_spread(norms[(s, "pre")])
                behind(7)

            def sublayer_out(s, name, per_tile, blocks, source, source_ready):
                first = stages[name][0]
                per_turn = 4 // per_tile

                def tile(n, turn, fresh):
                    if s or not fresh or n > 1:
                        pe.wait_ge(post_square, turn * per_turn + (DK * s + n - 1))
                    for m in range(per_tile):
                        slot = first + n * per_tile + m
                        slot_ready(slot, turn * 4)
                        for k in range(blocks):
                            kk = m * blocks + k
                            if fresh and n == 0:
                                source_ready(kk)
                            hi, lo = source(kk)
                            last = products(4 + n % 2, slot, k * P, hi, lo, kk == 0, kk == per_tile * blocks - 1)
                        last.then_inc(slot_done, 1)

                for n in range(per_turn):
                    tile(n, 0, True)
                with pe.Fori(1, DK // per_turn) as turn:
                    for n in range(per_turn):
                        tile(n, turn, False)
                for n, (summed, count, source) in enumerate(((post_summed, DK * s + DK, square_sum), (post_square, DK * (s + 1), square[1]))):
                    pe.wait_ge(summed, count)
                    for c in range(NC):
                        last = nc.tensor.matmul(ps[:, NORM, c:c + 1], source[:, c * P:c * P + P], ones[:, 0:1],
                                                start=n == 0 and c == 0, stop=n == 1 and c == NC - 1)
                last.then_inc(sums_ready, 1)
                norm_spread(norms[(s, "post")])

            def ffn(f, s):
                name = f"gate_up{f}"
                first = stages[name][0]
                first_four(s, name, 0)
                with pe.Fori(1, FT // 2) as turn:
                    for m in range(4):
                        if m % 2 == 0:
                            pe.wait_ge(up_scaled, turn * 2 + (FT * f + m // 2 - 1))
                        slot_ready(first + m, turn * 4)
                        for k in range(DK):
                            last = products(m, first + m, k * P, h_hi[:, k, :], h_lo[:, k, :], k == 0, k == DK - 1)
                        last.then_inc(slot_done, 1)
                sublayer_out(s, f"down{f}", 2, HALF, lambda k: (a_hi[:, k, :], a_lo[:, k, :]),
                             lambda k: pe.wait_ge(a_lo_ready, FT * f + k + 1))

            def projection(name, first_tile, done=0, until=None):
                first, slots, _ = stages[name]
                slots = until or slots

                def tile(n, turns):
                    bank = (first_tile + n) % 4
                    slot_ready(first + n, turns * 4)
                    pe.wait_ge(tile_taken, turns * 4 + (first_tile + n - 3))
                    for k in range(DK):
                        last = products(bank, first + n, k * P, h_hi[:, k, :], h_lo[:, k, :], k == 0, k == DK - 1)
                    last.then_inc(slot_done, 1)

                turns = (slots - done) // 4
                if turns > 1:
                    with pe.Fori(0, turns) as turn:
                        for n in range(4):
                            tile(done + n, turn)
                else:
                    turns = 0
                for n in range(done + 4 * turns, slots):
                    tile(n, 0)

            def tiles_of(name, tile0, banks, turn):
                first, at = stages[name][0], [0]

                def some(count):
                    for _ in range(count):
                        n, k = divmod(at[0], DK)
                        at[0] += 1
                        if k == 0:
                            slot_ready(first + n, turn * 4)
                            pe.wait_ge(tile_taken, turn * 4 + (tile0 + n - 1))
                        last = products(banks[n % 2], first + n, k * P, h_hi[:, k, :], h_lo[:, k, :], k == 0, k == DK - 1)
                        if k == DK - 1:
                            last.then_inc(slot_done, 1)

                return some

            def even():
                s = EVEN
                first_four(s, "qk_small", QK0)
                projection("qk_small", QK0, 4, 5)
                pe.wait_ge(even_in, 48)
                pe.wait_ge(tile_taken, QK0 + 1)
                for h in range(GH):
                    last = nc.tensor.matmul(ps[:, 4 + h, :], gate2[:, h * P:h * P + P], small[0:RANK, :], start=True, stop=True)
                last.then_inc(decay_logits, 1)
                projection("qk_small", QK0, 5)
                first = stages["v"][0]
                with pe.Fori(0, 2) as half:
                    for n in range(4):
                        slot_ready(first + n, half * 4)
                        slot = (first + n) % RING
                        for m in range(2):
                            k = 2 * n + m
                            w_h, w_l = w_hi[slot][:, m * T:m * T + T], w_lo[slot][:, m * T:m * T + T]
                            for c in range(NC):
                                bank = (V0 + c) % 4
                                if k == 0:
                                    pe.wait_ge(tile_taken, half * 4 + (V0 + c - 3))
                                h_h, h_l = h_hi[:, k, c * P:c * P + P], h_lo[:, k, c * P:c * P + P]
                                nc.tensor.matmul(ps[:, bank, :], h_h, w_h, start=k == 0, stop=False)
                                nc.tensor.matmul(ps[:, bank, :], h_h, w_l, start=False, stop=False)
                                last = nc.tensor.matmul(ps[:, bank, :], h_l, w_h, start=False, stop=k == DK - 1)
                        last.then_inc(slot_done, 1)
                turn_dt()
                gla_heads()
                ssm_groups()
                sublayer_out(s, "even_out", 2, 8, lambda k: (cat_hi[:, k, :], cat_lo[:, k, :]),
                             lambda k: pe.wait_ge(cat_lo_ready, k + 1))

            def turn_dt():
                pe.wait_ge(dt_far, 1)
                for n in range(14):
                    if n < 8:
                        source = (dt_rows if n < 4 else cum)[:, (n % 4) * P:(n % 4) * P + P]
                    else:
                        jc, ic = FAR[n - 8]
                        source = {1: far1[:, jc * P:jc * P + P], 2: far2[:, jc * P:jc * P + P], 3: far2[:, 2 * P:3 * P]}[ic - jc]
                    last = nc.tensor.matmul(ps[:, 4, n * SH:n * SH + SH], source, ident[DT0:DT0 + SH, DT0:DT0 + SH], start=True, stop=True)
                last.then_inc(cols_turned, 1)

            def gla_heads():
                pe.wait_ge(cols_ready, 1)
                with pe.Fori(0, GH) as h:
                    project = tiles_of("xbc", XBC0, XBC_BANKS, h)
                    project(8)
                    for j in range(len(SPANS)):
                        pe.wait_ge(gla_factors, h * 8 + (j + 1))
                        if j >= 2:
                            pe.wait_ge(gla_merged, h * 8 + (j - 1))
                        for c in range(NC):
                            queries = slice(c * HALF_P, c * HALF_P + HALF_P)
                            last = nc.tensor.matmul(ps[:, j % 2, queries], k_dec[j % 2][:, c * P:c * P + P], other[j % 2][:, queries],
                                                    start=True, stop=True)
                        last.then_inc(gla_products, 1)
                        project(2)
                    pe.wait_ge(key_copied, h + 1)
                    pe.wait_ge(gla_merged, h * 8 + 6)
                    q = rows(a_rows, h + Q)
                    for c in range(NC):
                        cols = slice(c * P, c * P + P)
                        last = nc.tensor.matmul(ps[:, 1, cols], k_dec[1][:, cols], q[:, cols], start=True, stop=True)
                    last.then_inc(gla_products, 1)
                    project(2)
                    pe.wait_ge(gla_factors, h * 8 + 8)
                    for (jc, ic) in FAR:
                        key = {1: k_dec[0][:, jc * P:jc * P + P], 2: k_dec[1][:, jc * P:jc * P + P], 3: k_dec[1][:, 2 * P:3 * P]}[ic - jc]
                        bank, at = ((4, ic - 1) if jc == 0 else (5, ic - 2 if jc == 1 else 2))
                        last = nc.tensor.matmul(ps[:, bank, at * P:at * P + P], key, other[0][:, ic * P:ic * P + P], start=True, stop=True)
                    last.then_inc(gla_products, 1)
                    project(3)
                    pe.wait_ge(gla_merged, h * 8 + 8)
                    pe.wait_ge(far_taken, h + 1)
                    pe.wait_ge(value_copied, h + 1)
                    for m in range(2):
                        for jc in range(NC):
                            value = v_head[jc][:, m * P:m * P + P]
                            last = nc.tensor.matmul(ps[:, 4 + m, jc * P:jc * P + P], value, scores[:, jc, :], start=jc == 0, stop=jc == NC - 1)
                            if jc < NC - 1:
                                nc.tensor.matmul(ps[:, 4 + m, (jc + 1) * P:T], value, far_blocks[jc], start=False, stop=False)
                    last.then_inc(gla_out, 1)
                    project(3)
                    norm_sums(head_summed, h + 1)
                    project(2)
                    norm_spread(h + norms[("gla", 0)])

            def ssm_groups():
                with pe.Fori(0, SG) as g:
                    project = tiles_of("zg", ZG0, ZG_BANKS, g)
                    project(8)
                    pe.wait_ge(group_copied, g + 1)
                    for c in range(NC):
                        for m in range(2):
                            at = ((c % 2) * 2 + m) * P
                            last = nc.tensor.transpose(ps[:, (0, 4)[c // 2], at:at + P], xs_group[:, m, c * P:c * P + P], ident[:, :])
                    last.then_inc(x_turned, 1)
                    c_row = rows(a_rows, g + C_ROWS)
                    for jc, (bank, at) in enumerate(CB_AT):
                        last = nc.tensor.matmul(ps[:, bank, at:at + T - jc * P], b_group[:, jc * P:jc * P + P], c_row[:, jc * P:T], start=True, stop=True)
                    last.then_inc(cb_ready, 1)
                    project(2)

                    def spread_row(r):
                        pe.wait_ge(head_row_ready, g * 4 + (r + 1))
                        if r == 0:
                            pe.wait_ge(x_taken, g + 1)
                        elif r == 1:
                            pe.wait_ge(cb_taken, g + 1)
                            pe.wait_ge(cb_far_taken, g + 1)
                        else:
                            pe.wait_ge(decay_diff, g * 4 + (r - 1))
                            pe.wait_ge(from_start_ready, g * 4 + (r - 1))
                        nc.tensor.matmul(ps[:, ROW_BANKS[r % 2], :], ones[DT0:DT0 + SH, :], head_row[r % 2], start=True, stop=True).then_inc(row_spread, 1)

                    def near(r):
                        pe.wait_ge(decay_ready, g * 4 + (r + 1))
                        half = slice(64 * (r % 2), 64 * (r % 2) + 64)
                        for c in range(NC):
                            cols = slice(c * P, c * P + P)
                            last = nc.tensor.matmul(ps[half, 2 + r // 2, cols], x_group[c][:, r * 64:r * 64 + 64], decay[r % 2][:, cols],
                                                    start=True, stop=True)
                        last.then_inc(y_diag_done, 1)

                    def far(m):
                        for ic in range(1, NC):
                            for jc in range(ic):
                                at = (ic - jc - 1) * P
                                last = nc.tensor.matmul(ps[:, 4 + m, ic * P:ic * P + P], x_far[:, FAR.index((jc, ic)), m * P:m * P + P],
                                                        far_blocks[jc][:, at:at + P], start=jc == 0, stop=jc == ic - 1)
                        last.then_inc(y_far_done, 1)

                    spread_row(0)
                    spread_row(1)
                    project(5)
                    near(0)
                    spread_row(2)
                    project(2)
                    near(1)
                    spread_row(3)
                    pe.wait_ge(x_far_ready, g + 1)
                    far(0)
                    project(1)
                    near(2)
                    pe.wait_ge(decay_diff, g * 4 + 4)
                    pe.wait_ge(from_start_ready, g * 4 + 4)
                    far(1)
                    near(3)
                    project(9)
                    norm_sums(group_summed, g + 1)
                    project(2)
                    norm_spread(g + norms[("ssm", 0)])
                    project(3)

            def odd():
                s = ODD
                first_four(s, "latent", LATENT0)
                projection("latent", LATENT0, 4, 5)
                norm_sums(latent_summed, 1)
                projection("latent", LATENT0, 5)
                norm_spread(norms["q_latent"])

                def turn(j):
                    if j == 0:
                        pe.wait_ge(tile_taken, LATENT0 + 6)
                        pe.wait_ge(odd_in, 48)
                    else:
                        pe.wait_ge(q_taken, 3 * j)
                        pe.wait_ge(rope_taken, j)
                    source = rows(a_rows, LATENT + 5 if j == 0 else QROPE + j - 1)
                    nc.tensor.matmul(ps[:, 7, :], turn_mat, source, start=True, stop=True).then_inc(rope_turned, 1)

                first = stages["q_up"][0]
                for i in range(MH // 2):
                    slot_ready(first + i)
                    if i >= 2:
                        pe.wait_ge(q_taken, 3 * (i - 1))
                    for m in range(3):
                        if (i, m) == (0, 2):
                            norm_sums(latent_summed, 2)
                        if (i, m) == (1, 0):
                            norm_spread(norms["kv_latent"])
                        for k in range(QR):
                            pe.wait_ge(latent_lo_ready, k + 1)
                            last = products(3 * (i % 2) + m, first + i, (3 * m + k) * P, latent_hi[:, k, :], latent_lo[:, k, :], k == 0, k == QR - 1)
                    last.then_inc(slot_done, 1)
                first = stages["k_up"][0]
                pe.wait_ge(latent_lo_ready, QR + KR)
                for i in range(2):
                    slot_ready(first + i)
                    for m in range(4):
                        pe.wait_ge(q_taken, 12) if i == 0 else pe.wait_ge(k_taken, m + 1)
                        for k in range(KR):
                            last = products(m, first + i, (2 * m + k) * P, latent_hi[:, QR + k, :], latent_lo[:, QR + k, :], k == 0, k == KR - 1)
                    last.then_inc(slot_done, 1)
                turn(0)
                first = stages["v_up"][0]
                for i in range(2):
                    slot_ready(first + i)
                    slot = (first + i) % RING
                    for c in range(NC):
                        pe.wait_ge(k_taken, 5 + c) if i == 0 else pe.wait_ge(v_taken, c + 1)
                        for k in range(KR):
                            w_h, w_l = w_hi[slot][:, k * T:k * T + T], w_lo[slot][:, k * T:k * T + T]
                            l_h, l_l = latent_hi[:, QR + k, c * P:c * P + P], latent_lo[:, QR + k, c * P:c * P + P]
                            nc.tensor.matmul(ps[:, c, :], l_h, w_h, start=k == 0, stop=False)
                            nc.tensor.matmul(ps[:, c, :], l_h, w_l, start=False, stop=False)
                            last = nc.tensor.matmul(ps[:, c, :], l_l, w_h, start=False, stop=k == KR - 1)
                        if c == NC - 1:
                            last.then_inc(slot_done, 1)
                        if c % 2:
                            turn(2 * i + c // 2 + 1)

                pe.wait_ge(v_taken, 2 * NC)
                pe.wait_ge(rope_done, 1)

                def scores_of(i, n):
                    half = slice(64 * (n % 2), 64 * (n % 2) + 64)
                    k_row = rows(a_rows, i * 2 + (KN + n))
                    pe.wait_ge(q_copied, i * 2 + (n + 1))
                    if n:
                        pe.wait_ge(exp_done, i * 8 + 4 * n)
                    for qt in range(NC):
                        count = (qt + 1) * P
                        nc.tensor.matmul(ps[:, qt, 0:count], q_head[:, qt * P:qt * P + P], k_row[:, 0:count], start=True, stop=False)
                        nc.tensor.matmul(ps[:, qt, 0:count], q_pair[half, qt * P:qt * P + P], krope[half, 0:count],
                                         start=False, stop=True).then_inc(scores_done, 1)

                def values_of(i, n):
                    pe.wait_ge(probs_ready, i * 2 + (n + 1))
                    for kc in range(NC):
                        if kc >= 2:
                            pe.wait_ge(turned_act, i * 8 + (4 * n + kc - 1))
                        for qt in range(kc, NC):
                            last = nc.tensor.transpose(ps[:, 4 + kc % 2, qt * P:qt * P + P], probs[:, qt, kc * P:kc * P + P], ident[:, :])
                        last.then_inc(probs_turned, 1)
                    if n == 0:
                        pe.wait_ge(pair_copied, i + 1)
                    for kc in range(NC):
                        pe.wait_ge(turned_act, i * 8 + (4 * n + kc + 1))
                        last = nc.tensor.matmul(ps[:, 6 + n, kc * P:T], v_pair[:, kc, n * P:n * P + P], probs_t[:, kc, kc * P:T],
                                                start=kc == 0, stop=kc == NC - 1)
                    last.then_inc(att_done, 1)

                def pair(i, last):
                    scores_of(i, 1)
                    values_of(i, 0)
                    if not last:
                        scores_of(i, 2)
                    values_of(i, 1)

                scores_of(0, 0)
                with pe.Fori(0, MH // 2 - 1) as i:
                    pair(i, False)
                pair(MH // 2 - 1, True)
                sublayer_out(s, "odd_out", 1, 8, lambda k: (o_hi[:, k, :], o_lo[:, k, :]),
                             lambda k: pe.wait_ge(o_lo_ready, k + 1))

            pe.wait_ge(consts_in, 32)
            pe.wait_ge(consts_made, 2)
            for s in range(N_SUB):
                if s == EVEN:
                    even()
                elif s == ODD:
                    odd()
                else:
                    ffn(FFN_OF[s], s)

        @block.vector
        def _(dve):
            steps, offset = [0], [None]

            def signal(ins):
                steps[0] += 1
                ins.then_inc(dve_step, 1)

            def settle():
                dve.wait_ge(dve_step, steps[0] if offset[0] is None else offset[0] + steps[0])

            def after(ins):
                signal(ins)
                settle()

            @contextmanager
            def loop(turns, per_turn):
                before = steps[0]
                with dve.Fori(0, turns) as turn:
                    offset[0] = turn * per_turn
                    yield turn
                offset[0] = None
                assert steps[0] - before == per_turn, steps[0] - before
                steps[0] = before + per_turn * turns

            def tt(to, a, b, op):
                return nc.vector.tensor_tensor(to, a, b, op)

            def ts(to, a, s1, s2, op0, op1=ALU.bypass):
                return nc.vector.tensor_scalar(to, a, s1, s2, op0, op1) if s2 is not None else nc.vector.tensor_scalar(to, a, s1, None, op0)

            def stt(to, a, scalar, b, op0, op1):
                return nc.vector.scalar_tensor_tensor(out=to, in0=a, scalar=scalar, in1=b, op0=op0, op1=op1)

            def norm_mean(n, columns):
                dve.wait_ge(sums_ready, n + 1)
                ts(mean[:, :], ps[:, NORM, 0:NC], 1.0 / columns, EPS, ALU.mult, ALU.add).then_inc(mean_ready, 1)

            def norm_diagonals(n):
                dve.wait_ge(rstd_col_ready, n + 1)
                tt(diag, ident[:, :].unsqueeze(1).to_broadcast([P, NC, P]), rstd_col[:, :].unsqueeze(2).to_broadcast([P, NC, P]),
                   ALU.mult).then_inc(diag_ready, 1)

            def norm_copy(n, s, to=rstd[:, :]):
                dve.wait_ge(spread_ready, n + 1)
                nc.vector.tensor_copy(to, ps[:, NORM, :]).then_inc(rstd_ready, 1)
                dve.wait_ge(rstd_ready, n + (1 - s))

            def norm(n, columns, s, to=rstd[:, :]):
                norm_mean(n, columns)
                norm_diagonals(n)
                norm_copy(n, s, to)

            def add_update(s, k):
                dve.wait_ge(u_ready, DK * (s + 1))
                dve.wait_ge(spread_ready, norms[(s, "post")] + 1)
                after(tt(scaled[k % 2][:, :], u_row(s, k), ps[:, NORM, :], ALU.mult))
                tt(x[:, k, :], x[:, k, :], scaled[k % 2][:, :], ALU.add).then_inc(residual_ready, 1)

            def low_of_h(s, k):
                dve.wait_ge(h_hi_ready, DK * s + k + 1)
                stt(h_lo[:, k, :], x[:, k, :], pre_gain(s)[:, k:k + 1], h_hi[:, k, :].bitcast(F32),
                    ALU.mult, ALU.subtract).then_inc(h_lo_ready, 1)

            def pre_norm(s):
                for k in range(DK):
                    if s:
                        add_update(s - 1, k)
                    if k:
                        low_of_h(s, k - 1)
                low_of_h(s, DK - 1)
                norm(norms[(s, "pre")], D, s)

            def post_norm(s):
                nc.vector.memset(square_sum[:, :], 0.0).then_inc(post_summed, 1)
                for tile in range(DK - 1):
                    dve.wait_ge(post_square, DK * s + tile + 1)
                    dve.wait_ge(post_summed, DK * s + tile + 1)
                    tt(square_sum[:, :], square_sum[:, :], square[tile % 2][:, :], ALU.add).then_inc(post_summed, 1)
                norm_mean(norms[(s, "post")], D)
                norm_diagonals(norms[(s, "post")])

            def ffn(f, s):
                slot = stages[f"gate_up{f}"][0]

                def take(tile, b):
                    dve.wait_ge(slot_done, tile * 2 + (slot + 1))
                    tt(scaled[b][:, :], ps[:, 2 * b, :], rstd[:, :], ALU.mult).then_inc(gate_scaled, 1)
                    dve.wait_ge(slot_done, tile * 2 + (slot + 2))
                    tt(other[b][:, :], ps[:, 2 * b + 1, :], rstd[:, :], ALU.mult).then_inc(up_scaled, 1)
                    dve.wait_ge(silu_done, tile + (FT * f + 1))
                    dve.wait_ge(up_scaled, tile + (FT * f + 1))
                    tt(scaled[b][:, :], scaled[b][:, :], other[b][:, :], ALU.mult).then_inc(a_ready, 1)
                    dve.wait_ge(a_hi_ready, tile + (FT * f + 1))
                    tt(rows_r(a_lo, tile), scaled[b][:, :], rows_r(a_hi, tile).bitcast(F32), ALU.subtract).then_inc(a_lo_ready, 1)

                with dve.Fori(0, FT // 2) as turn:
                    for b in range(2):
                        take(turn * 2 + b, b)
                post_norm(s)

            def even():
                s = EVEN

                def take(n):
                    dve.wait_ge(slot_done, stages["qk_small"][0] + n + 1)
                    source = ps[:, (QK0 + n) % 4, :]
                    if 1 <= n <= GH:
                        stt(rows(a_rows, Q + n - 1), source, float(P) ** -0.5, rstd[:, :], ALU.mult, ALU.mult).then_inc(tile_taken, 1)
                    else:
                        tt(rows(a_rows, K + n - 1 - GH) if n else small, source, rstd[:, :], ALU.mult).then_inc(tile_taken, 1)

                def take_v(half):
                    dve.wait_ge(slot_done, stages["v"][0] + 4 * half + 4)
                    for c in range(NC):
                        ts(rows(a_rows, V + 2 * c + half), ps[:, (V0 + c) % 4, :], rstd_col[:, c:c + 1], None, ALU.mult).then_inc(tile_taken, 1)

                for n in range(5):
                    take(n)
                dve.wait_ge(decay_logits, 1)
                for h in range(GH):
                    row = rows(a_rows, LOG_A + h)
                    after(ts(row, ps[:, 4 + h, :], gla_bias[:, h:h + 1], None, ALU.add))
                    if h >= 2:
                        dve.wait_ge(softplus_ready, h - 1)
                        after(stt(rows(a_rows, LOG_A + h - 2), rows(a_rows, LOG_A + h - 2), 0.0, other[h % 2][:, :], ALU.min, ALU.subtract))
                    stt(other[h % 2][:, :], row, -1.0, row, ALU.mult, ALU.max).then_inc(logit_ready, 1)
                take(5)
                for h in (2, 3):
                    dve.wait_ge(softplus_ready, h + 1)
                    after(stt(rows(a_rows, LOG_A + h), rows(a_rows, LOG_A + h), 0.0, other[h % 2][:, :], ALU.min, ALU.subtract))
                take(6)
                after(ts(rows(a_rows, LOG_A, 4), rows(a_rows, LOG_A, 4), 1.0 / 16.0, None, ALU.mult))
                take(7)
                for h in range(GH):
                    for c in range(NC):
                        part = rows(a_rows, LOG_A + h)[:, c * P:c * P + P]
                        last = nc.vector.tensor_tensor_scan(part, ones[:, :], part, 0.0, ALU.mult, ALU.add)
                    last.then_inc(log_a_ready, 1)
                take(8)
                step_sizes()
                take_v(0)
                take_v(1)
                dve.wait_ge(cols_turned, 1)
                nc.vector.tensor_copy(ssm_cols[:, :, :].rearrange("p n h -> p (n h)"), ps[:, 4, 0:14 * SH]).then_inc(cols_ready, 1)
                dve.wait_ge(cols_ready, 1)
                gla_heads()
                dve.wait_ge(conv_done, 16)
                ssm_groups()
                for k in range(len(CAT)):
                    dve.wait_ge(cat_hi_ready, k + 1)
                    tt(cat_lo[:, k, :], rows(a_rows, CAT[k]), cat_hi[:, k, :].bitcast(F32), ALU.subtract).then_inc(cat_lo_ready, 1)
                post_norm(s)

            def step_sizes():
                dt_raw = small[DT0:DT0 + SH, :]
                after(ts(dt_rows, dt_raw, dt_bias, None, ALU.add))
                stt(far1, dt_rows, -1.0, dt_rows, ALU.mult, ALU.max).then_inc(dt_signal, 1)
                dve.wait_ge(dt_act, 1)
                ts(far2, far1, 1.0, None, ALU.add).then_inc(dt_signal, 1)
                dve.wait_ge(dt_act, 2)
                after(stt(far2, far2, 1.0, far1, ALU.subtract, ALU.subtract))
                after(tt(cum, cum, far2, ALU.subtract))
                after(stt(dt_rows, dt_rows, 0.0, cum, ALU.max, ALU.add))
                after(ts(cum, dt_rows, a_log, -1.0, ALU.mult, ALU.mult))
                for c in range(NC):
                    part = cum[:, c * P:c * P + P]
                    last = nc.vector.tensor_tensor_scan(part, ones[DT0:DT0 + SH, :], part, 0.0, ALU.mult, ALU.add)
                last.then_inc(dt_cum, 1)
                dve.wait_ge(dt_cum, 1)
                chunks = cum.rearrange("p (c t) -> p c t", c=NC)[:, 0:3, :]
                tt(far1[:, 0:3 * P].rearrange("p (c t) -> p c t", c=3), chunks[:, :, P - 1:P].to_broadcast([SH, 3, P]),
                   chunks, ALU.subtract).then_inc(dt_cum, 1)
                dve.wait_ge(dt_act, 3)
                ts(far2[:, P:2 * P], far1[:, P:2 * P], ssm_chunk_decay[:, 2:3], None, ALU.mult)
                after(ts(far2[:, 0:P], far1[:, 0:P], ssm_chunk_decay[:, 1:2], None, ALU.mult))
                ts(far2[:, 2 * P:3 * P], far2[:, 0:P], ssm_chunk_decay[:, 2:3], None, ALU.mult).then_inc(dt_far, 1)

            def gla_heads():
                dve.wait_ge(even_in, 48)
                nc.vector.tensor_copy(level_mask, rows(a_rows, XS, 2)[:, 0:MASKS])
                for buffer in k_dec:
                    nc.vector.memset(buffer, 0.0)
                after(nc.vector.memset(rows(a_rows, 33), 0.0))
                with loop(GH, 4) as h:
                    log_a, q, k = rows(a_rows, h + LOG_A), rows(a_rows, h + Q), rows(a_rows, h + K)

                    def take(n):
                        dve.wait_ge(slot_done, h * 4 + (stages["xbc"][0] + n + 1))
                        if n >= 2:
                            dve.wait_ge(conv_done, h * 4 + (n - 1))
                        tt(conv_in[n % 2], ps[:, XBC_BANKS[n % 2], :], rstd[:, :], ALU.mult).then_inc(tile_taken, 1)

                    def tap(n, back):
                        if back == 1 and n < 3:
                            dve.wait_ge(conv_started, h * 3 + (n + 1))
                        elif back > 1:
                            dve.wait_ge(conv_step, h * 8 + (2 * n + back - 1))
                        row = rows(a_rows, h * 4 + (XS + n), 1)
                        to = row[:, back:T]
                        stt(to, conv_in[n % 2][:, 0:T - back], mixer_cols[:, ds(h * 16 + (4 * n + 3 - back), 1)], to,
                            ALU.mult, ALU.add).then_inc(conv_step if back < 3 else conv_done, 1)

                    def differences(j):
                        span = SPANS[j]
                        blocks = log_a.rearrange("p (n w t) -> p n w t", w=2, t=span)
                        to = scaled[j % 2][:, :].rearrange("p (n w t) -> p n w t", w=2, t=span)
                        if j >= 2:
                            dve.wait_ge(gla_factors, h * 8 + (j - 1))
                        middle = blocks[:, :, 0, span - 1:span].to_broadcast([P, T // (2 * span), span])
                        tt(to[:, :, 0, :], middle, blocks[:, :, 0, :], ALU.subtract)
                        tt(to[:, :, 1, :], blocks[:, :, 1, :], middle, ALU.subtract).then_inc(gla_diff, 1)

                    def factors(j):
                        dve.wait_ge(gla_decay, h * 8 + (j + 1))
                        if j >= 2:
                            dve.wait_ge(gla_products, h * 9 + (j - 1))
                        if j >= 3:
                            dve.wait_ge(gla_merged, h * 8 + (j - 2))

                        def half(row, w):
                            return row.rearrange("p (n w t) -> p n w t", w=2, t=SPANS[j])[:, :, w, :]

                        tt(other[j % 2][:, 0:T // 2].rearrange("p (n t) -> p n t", t=SPANS[j]), half(q, 1), half(scaled[j % 2][:, :], 1), ALU.mult)
                        tt(half(k_dec[j % 2], 0), half(k, 0), half(scaled[j % 2][:, :], 0), ALU.mult).then_inc(gla_factors, 1)

                    def merge(j):
                        if j < len(SPANS):
                            span = SPANS[j]
                            to = scores.rearrange("p c (n w t) -> p c n w t", w=2, t=span)[:, :, :, 1, :]
                            mask = level_mask[:, j * HALF_P:(j + 1) * HALF_P]
                            source = ps[:, j % 2, 0:T // 2].rearrange("p (c n t) -> p c n t", c=NC, t=span)
                            shape = [P, NC, HALF_P // span, span]
                            mask = mask.rearrange("p (n t) -> p n t", t=span).unsqueeze(1).to_broadcast(shape)
                        else:
                            to, mask = scores, level_mask[:, MASKS - P:MASKS].unsqueeze(1).to_broadcast([P, NC, P])
                            source = ps[:, 1, :].rearrange("p (c t) -> p c t", c=NC)
                        nc.vector.copy_predicated(to, mask, source).then_inc(gla_merged, 1)

                    for j in range(len(SPANS) + 1):
                        if j < len(SPANS):
                            differences(j)
                        if j == 3:
                            tap(0, 1)
                        if j:
                            factors(j - 1)
                        if j == len(SPANS):
                            chunks = log_a.rearrange("p (c t) -> p c t", c=NC)[:, 0:3, :]
                            dve.wait_ge(gla_factors, h * 8 + 7)
                            tt(scaled[0][:, 0:3 * P].rearrange("p (c t) -> p c t", c=3), chunks[:, :, P - 1:P].to_broadcast([P, 3, P]),
                               chunks, ALU.subtract).then_inc(gla_diff, 1)
                        if j >= 3:
                            merge(j - 3)
                        if j == 2:
                            take(0)
                        if j == 4:
                            tap(0, 2)
                        if j == 5:
                            tap(0, 3)
                        if j == 6:
                            take(1)
                    dve.wait_ge(gla_decay, h * 8 + 8)
                    dve.wait_ge(gla_products, h * 9 + 7)
                    dve.wait_ge(gla_merged, h * 8 + 5)
                    tt(other[0][:, P:T], q[:, P:T], scaled[1][:, P:T], ALU.mult)
                    merge(5)
                    dve.wait_ge(gla_merged, h * 8 + 6)
                    signal(tt(k_dec[0][:, 0:3 * P], k[:, 0:3 * P], scaled[0][:, 0:3 * P], ALU.mult))
                    merge(6)
                    settle()
                    dve.wait_ge(gla_merged, h * 8 + 7)
                    dve.wait_ge(gla_products, h * 9 + 8)
                    ts(k_dec[1][:, P:2 * P], k_dec[0][:, P:2 * P], chunk_decay[:, 2:3], None, ALU.mult)
                    after(ts(k_dec[1][:, 0:P], k_dec[0][:, 0:P], chunk_decay[:, 1:2], None, ALU.mult))
                    ts(k_dec[1][:, 2 * P:3 * P], k_dec[1][:, 0:P], chunk_decay[:, 2:3], None, ALU.mult).then_inc(gla_factors, 1)
                    merge(7)
                    tap(1, 1)
                    take(2)
                    tap(1, 2)
                    tap(2, 1)
                    tap(1, 3)
                    tap(2, 2)
                    dve.wait_ge(head_squares, h + 1)
                    tt(square_sum[:, :], square_sum[:, :], other[0][:, :], ALU.add).then_inc(head_summed, 1)
                    tap(2, 3)
                    norm_mean(h + norms[("gla", 0)], GDV)
                    take(3)
                    norm_diagonals(h + norms[("gla", 0)])
                    dve.wait_ge(tile_taken, h * 4 + (XBC0 + 4))
                    signal(ts(rows(a_rows, h * 4 + (XS + 3)), conv_in[1], mixer_cols[:, ds(h * 16 + 15, 1)],
                              mixer_cols[:, ds(h * 4 + 67, 1)], ALU.mult, ALU.add))
                    norm_copy(h + norms[("gla", 0)], EVEN, head_rstd)
                    for m, row in enumerate((q, k)):
                        last = stt(row, ps[:, 4 + m, :], gla_gain[:, m:m + 1], head_rstd, ALU.mult, ALU.mult)
                    after(last)
                    for back in (1, 2, 3):
                        tap(3, back)

            def ssm_groups():
                with loop(SG, 5) as g:
                    heads = ds(g * 4, 4)

                    def take(n):
                        dve.wait_ge(slot_done, g * 4 + (stages["zg"][0] + n + 1))
                        tt(scaled[n % 2][:, :], ps[:, ZG_BANKS[n % 2], :], rstd[:, :], ALU.mult).then_inc(tile_taken, 1)

                    def head_row_of(r):
                        if r >= 2:
                            dve.wait_ge(row_spread, g * 4 + (r - 1))
                        ts(head_row[r % 2], cum, ident[DT0:DT0 + SH, ds(g * 4 + (DT0 + r), 1)], None, ALU.mult).then_inc(head_row_ready, 1)

                    def difference(r):
                        dve.wait_ge(from_start_ready, g * 4 + (r + 1))
                        if r >= 2:
                            dve.wait_ge(y_diag_done, g * 4 + (r - 1))
                        for c in range(NC):
                            last = ts(decay[r % 2][:, c * P:c * P + P], ps[:, ROW_BANKS[r % 2], c * P:c * P + P],
                                      ssm_cols[:, 4 + c, ds(g * 4 + r, 1)], 0.0, ALU.subtract, ALU.min)
                        last.then_inc(decay_diff, 1)

                    def with_cb(r):
                        dve.wait_ge(decay_exp, g * 4 + (r + 1))
                        blocks = decay[r % 2].rearrange("p (c t) -> p c t", c=NC)
                        tt(blocks, blocks, cb, ALU.mult).then_inc(decay_ready, 1)

                    head_row_of(0)
                    head_row_of(1)
                    dve.wait_ge(x_turned, g + 1)
                    for c in range(NC):
                        dt_cols = ssm_cols[:, c, heads].unsqueeze(2).to_broadcast([P, 4, SV])
                        last = tt(x_group[c].rearrange("p (h v) -> p h v", h=4),
                                  ps[:, (0, 4)[c // 2], (c % 2) * 256:(c % 2) * 256 + 256].rearrange("p (h v) -> p h v", h=4), dt_cols, ALU.mult)
                    last.then_inc(x_taken, 1)
                    dve.wait_ge(x_taken, g + 1)
                    dve.wait_ge(cb_far_taken, g + 1)
                    for jc, (bank, at) in enumerate(CB_AT):
                        last = tt(cb[:, jc, :], ps[:, bank, at:at + P], tri, ALU.mult)
                    last.then_inc(cb_taken, 1)
                    dve.wait_ge(cb_taken, g + 1)
                    difference(0)
                    head_row_of(2)
                    difference(1)
                    head_row_of(3)
                    with_cb(0)
                    with_cb(1)
                    for n, (jc, ic) in enumerate(FAR):
                        cols = ssm_cols[:, 8 + n, heads].unsqueeze(2).to_broadcast([P, 4, SV])
                        last = tt(x_far[:, n, :].rearrange("p (h v) -> p h v", h=4), x_group[jc].rearrange("p (h v) -> p h v", h=4),
                                  cols, ALU.mult)
                    last.then_inc(x_far_ready, 1)
                    take(0)
                    difference(2)

                    def outputs(m):
                        dve.wait_ge(y_far_done, g * 2 + (m + 1))
                        dve.wait_ge(y_diag_done, g * 4 + (2 * m + 2))
                        dve.wait_ge(from_start_ready, g * 4 + (2 * m + 2))
                        tt(other[m][:, P:T], ps[:, 4 + m, P:T], from_start[m][:, P:T], ALU.mult)
                        after(stt(y_sum[m], xs_group[:, m, :], mixer_cols[:, ds(g * 2 + (86 + m), 1)], ps[:, 2 + m, :], ALU.mult, ALU.add))
                        after(tt(y_sum[m][:, P:T], y_sum[m][:, P:T], other[m][:, P:T], ALU.add))

                    def gate(m):
                        dve.wait_ge(row_silu, g * 4 + (m + 1))
                        tt(rows(a_rows, g * 2 + (XS + m)), y_sum[m], scaled[m][:, :], ALU.mult).then_inc(y_gated, 1)

                    difference(3)
                    with_cb(2)
                    take(1)
                    with_cb(3)
                    outputs(0)
                    gate(0)
                    outputs(1)
                    dve.wait_ge(y_gated, g * 2 + 1)
                    take(2)
                    gate(1)
                    dve.wait_ge(group_squares, g + 1)
                    tt(square_sum[:, :], square_sum[:, :], other[0][:, :], ALU.add).then_inc(group_summed, 1)
                    norm(g + norms[("ssm", 0)], 256, EVEN, head_rstd)
                    for m in range(2):
                        row = rows(a_rows, g * 2 + (XS + m))
                        last = stt(row, row, mixer_cols[:, ds(g * 2 + (94 + m), 1)], head_rstd, ALU.mult, ALU.mult)
                    after(last)
                    take(3)
                    for m in range(2):
                        dve.wait_ge(row_silu, g * 4 + (m + 3))
                        row = rows(a_rows, g + (Q + GH * m))
                        last = tt(row, row, scaled[m][:, :], ALU.mult)
                    last.then_inc(group_done, 1)

            def odd():
                s = ODD
                def take(n):
                    dve.wait_ge(slot_done, stages["latent"][0] + n + 1)
                    tt(rows(a_rows, LATENT + n), ps[:, (LATENT0 + n) % 4, :], rstd[:, :], ALU.mult).then_inc(tile_taken, 1)

                def sum_squares(start, count):
                    for m in range(1, count):
                        dve.wait_ge(latent_square, start + m + 1)
                        last = tt(square_sum[:, :], square_sum[:, :], other[m - 1][:, :], ALU.add)
                        if m < count - 1:
                            after(last)
                    last.then_inc(latent_summed, 1)

                def normalise(start, count, row):
                    for n in range(start, start + count):
                        stt(rows(a_rows, LATENT + n), rows(a_rows, LATENT + n), latent_gain[:, n:n + 1], row,
                            ALU.mult, ALU.mult).then_inc(latent_normed, 1)
                    for n in range(start, start + count):
                        dve.wait_ge(latent_hi_ready, n + 1)
                        tt(latent_lo[:, n, :], rows(a_rows, LATENT + n), latent_hi[:, n, :].bitcast(F32), ALU.subtract).then_inc(latent_lo_ready, 1)

                for n in range(4):
                    take(n)
                sum_squares(0, QR)
                take(4)
                norm_mean(norms["q_latent"], QR * P)
                norm_diagonals(norms["q_latent"])
                take(5)
                norm_copy(norms["q_latent"], ODD, cos)
                normalise(0, QR, cos)
                sum_squares(QR, KR)
                norm(norms["kv_latent"], KR * P, ODD, sin)
                normalise(QR, KR, sin)

                dve.wait_ge(odd_in, 48)
                after(nc.vector.tensor_copy(angle[1], angle[0].bitcast(I32)))
                after(ts(angle[0], angle[1], inv_freq, None, ALU.mult))
                for n, quarter in enumerate((0.0, 0.25)):
                    if n:
                        dve.wait_ge(table_ready, 1)
                    after(ts(angle[2], angle[0], 1.0 / (2.0 * np.pi), quarter, ALU.mult, ALU.add))
                    after(ts(angle[2], angle[2], ROUND, ROUND, ALU.add, ALU.subtract))
                    after(stt(angle[1], angle[2], -TURN[0], angle[0], ALU.mult, ALU.add))
                    after(stt(angle[1], angle[2], -TURN[1], angle[1], ALU.mult, ALU.add))
                    after(stt(angle[1], angle[2], -TURN[2], angle[1], ALU.mult, ALU.add))
                    after(ts(angle[1], angle[1], quarter * 2.0 * np.pi, PI_BELOW, ALU.add, ALU.min))
                    ts(angle[1], angle[1], -PI_BELOW, None, ALU.max).then_inc(angle_ready, 1)

                def rotate(j):
                    source = rows(a_rows, LATENT + 5 if j == 0 else QROPE + j - 1)
                    to = krope if j == 0 else source
                    dve.wait_ge(table_ready, 2)
                    dve.wait_ge(rope_turned, j + 1)
                    if j:
                        dve.wait_ge(rope_done, j)
                    tt(other[1][:, :], ps[:, 7, :], sin, ALU.mult).then_inc(rope_taken, 1)
                    after(tt(other[0][:, :], source, cos, ALU.mult))
                    tt(to, other[0][:, :], other[1][:, :], ALU.add).then_inc(rope_done, 1)

                slot = stages["k_up"][0]
                for i in range(2):
                    dve.wait_ge(slot_done, slot + i + 1)
                    for m in range(4):
                        nc.vector.tensor_copy(rows(a_rows, KN + 4 * i + m), ps[:, m, :]).then_inc(k_taken, 1)
                for j in range(1 + MH // 2):
                    rotate(j)

                def maxima(i, n):
                    dve.wait_ge(scores_done, i * 8 + (4 * n + 4))
                    near = diagonal(ps[:, 0:NC, :].rearrange("p i (j t) -> p i j t", t=P))
                    after(tt(near, near, causal.unsqueeze(1).to_broadcast([P, NC, P]), ALU.add))
                    for qt in range(NC):
                        last = nc.vector.reduce_max(peak[:, qt:qt + 1], ps[:, qt, 0:(qt + 1) * P], AX_X)
                    after(last)
                    ts(peak_bias, peak, -SCORE_SCALE, None, ALU.mult).then_inc(bias_ready, 1)

                def pair(i, last):
                    for n in range(2):
                        dve.wait_ge(exp_done, i * 8 + (4 * n + 4))
                        after(nc.vector.reciprocal(prob_sum, prob_sum))
                        for qt in range(NC):
                            ins = ts(probs[:, qt, 0:(qt + 1) * P], probs[:, qt, 0:(qt + 1) * P], prob_sum[:, qt:qt + 1], None, ALU.mult)
                        ins.then_inc(probs_ready, 1)
                        if not last or n == 0:
                            maxima(i, n + 1)
                        dve.wait_ge(o_hi_ready, i * 2 + (n + 1))
                        tt(rows_r(o_lo, i * 2 + n), ps[:, 6 + n, :], rows_r(o_hi, i * 2 + n).bitcast(F32), ALU.subtract).then_inc(o_lo_ready, 1)

                maxima(0, 0)
                with loop(MH // 2 - 1, 2 * 3) as i:
                    pair(i, False)
                pair(MH // 2 - 1, True)
                post_norm(s)

            dve.wait_ge(gains_in, 16)
            dve.wait_ge(consts_in, 32)
            for s in range(N_SUB):
                if s not in (EVEN, ODD):
                    last = ts(post_gain(s), post_gain(s), 0.5, None, ALU.mult)
            last.then_inc(gains_halved, 1)
            for s in range(N_SUB):
                pre_norm(s)
                if s == EVEN:
                    even()
                elif s == ODD:
                    odd()
                else:
                    ffn(FFN_OF[s], s)
            for k in range(DK):
                add_update(N_SUB - 1, k)


def blocks_of(w):
    k, n = w.shape
    return w.reshape(k // P, P, n // P, P).transpose(2, 1, 0, 3).reshape(n // P, P, k)


def halves_of(blocks):
    n, _, k = blocks.shape
    return blocks.reshape(n, P, 2, k // 2).transpose(0, 2, 1, 3).reshape(2 * n, P, k // 2)


def merged(blocks, count):
    n, _, k = blocks.shape
    return blocks.reshape(n // count, count, P, k).transpose(0, 2, 1, 3).reshape(n // count, P, count * k)


def moving_of(w, per_slot):
    k, n = w.shape
    return (w.reshape(k // P // per_slot, per_slot, P, n // T, T).transpose(3, 0, 2, 1, 4)
            .reshape(-1, P, per_slot * T))


def columns_of(v):
    return v.reshape(-1, P).T


def constants():
    j, i = np.arange(P)[:, None], np.arange(P)[None, :]
    levels = [((j // (2 * n) == i // (2 * n)) & (j // n % 2 == 0))[:, i[0] // n % 2 == 1] for n in SPANS] + [j == i]
    turn = np.where(j % ROPE == i % ROPE + ROPE // 2, -1.0, 0.0) + np.where(j % ROPE + ROPE // 2 == i % ROPE, 1.0, 0.0)
    frequencies = (10000.0 ** (-np.arange(0, ROPE, 2, dtype=np.float32) / ROPE)).astype(np.float32)
    return {
        "ident": np.eye(P, dtype=np.float32),
        "level_mask": np.concatenate(levels, axis=1).astype(np.float32),
        "tri": (j <= i).astype(np.float32),
        "causal": np.where(i <= j, 0.0, -1e30).astype(np.float32),
        "turn": (turn * (j // ROPE == i // ROPE)).astype(np.float32),
    }, np.tile(frequencies, 4)


def lay_out(a):
    arrays, frequencies = constants()
    names = [[f"{part}_{when}_norm" for part in ("ffn1", "mix", "ffn2")] for when in ("pre", "post")]
    arrays["gains"] = np.concatenate([columns_of(a[n][layer]) for group in names for layer in range(2) for n in group], axis=1)
    arrays["x_t"] = a["x"][0].T
    arrays["positions"] = a["positions"]
    for f in range(N_FFN):
        ffn, layer = ("ffn1", "ffn2")[f % 2], f // 2
        gate, up = blocks_of(a[ffn + "_w_gate"][layer]), blocks_of(a[ffn + "_w_up"][layer])
        arrays[f"w_gate_up{f}"] = np.stack([gate, up], axis=1).reshape(2 * FT, P, D)
        arrays[f"w_down{f}"] = halves_of(blocks_of(a[ffn + "_w_down"][layer]))

    w_in = a["ab_w_in"][0]
    sizes = (GH * P, GH * P, GH * GDV, GH * GDV, RANK, SH * SV, SH * SV + 2 * SG * P, SH)
    q, k, v, g, a_low, z, xbc, dt = np.split(w_in, np.cumsum(sizes)[:-1], axis=1)
    small = np.zeros((D, P), np.float32)
    small[:, 0:RANK] = a_low
    small[:, DT0:DT0 + SH] = dt
    arrays["w_qk_small"] = blocks_of(np.concatenate([small, q, k], axis=1))
    arrays["w_v"] = moving_of(v, 2)
    arrays["w_xbc"] = blocks_of(xbc)
    zg = [blocks_of(u).reshape(SG, 2, P, D) for u in (z, g)]
    arrays["w_zg"] = np.concatenate(zg, axis=1).reshape(4 * SG, P, D)
    w_out = a["ab_w_out"][0]
    gla_out = w_out[:GH * GDV].reshape(GH, 2, P, D).transpose(1, 0, 2, 3).reshape(GH * GDV, D)
    arrays["w_even_out"] = halves_of(blocks_of(np.concatenate([gla_out, w_out[GH * GDV:]])))
    arrays["gate2"] = a["gla_w_gate2"][0]

    down = a["mla_w_down"][0]
    arrays["w_latent"] = blocks_of(np.concatenate([down, down[:, (QR + KR) * P:]], axis=1))
    uq = a["mla_w_uq"][0].reshape(QR * P, MH, P + ROPE)
    pairs = [np.concatenate([uq[:, 2 * i, :P], uq[:, 2 * i + 1, :P], uq[:, 2 * i, P:], uq[:, 2 * i + 1, P:]], axis=1) for i in range(MH // 2)]
    arrays["w_q_up"] = merged(blocks_of(np.concatenate(pairs, axis=1)), 3)
    ukv = a["mla_w_ukv"][0].reshape(KR * P, MH, 2 * P)
    arrays["w_k_up"] = merged(blocks_of(ukv[:, :, :P].reshape(KR * P, MH * P)), 4)
    arrays["w_v_up"] = moving_of(ukv[:, :, P:].reshape(KR * P, MH * P), 2)
    arrays["w_odd_out"] = blocks_of(a["mla_w_o"][0])

    cols = np.zeros((P, 110), np.float32)
    cols[:, 0:64] = a["ssm_conv_w"][0].reshape(4, 16, P).transpose(2, 1, 0).reshape(P, 64)
    cols[:, 64:80] = columns_of(a["ssm_conv_b"][0])
    cols[:, 80:84] = columns_of(a["gla_b_gate2"][0])
    cols[:, 84:86] = columns_of(a["gla_norm"][0])
    cols[:, 86:94] = np.repeat(a["ssm_d"][0], SV).reshape(8, P).T
    cols[:, 94:102] = columns_of(a["ssm_norm"][0])
    cols[DT0:DT0 + SH, 102] = a["ssm_dt_bias"][0]
    cols[DT0:DT0 + SH, 103] = a["ssm_a_log"][0]
    cols[:, 104:107] = columns_of(a["mla_q_norm"][0])
    cols[:, 107:109] = columns_of(a["mla_kv_norm"][0])
    cols[:, 109] = frequencies
    arrays["mixer_cols"] = cols
    return {k: np.ascontiguousarray(v) for k, v in arrays.items()}


def kernel(**inputs):
    import concourse.bacc as bacc
    from concourse.bass_utils import run_bass_kernel_spmd

    arrays = lay_out({k: np.asarray(v) for k, v in inputs.items()})
    nc = bacc.Bacc("TRN2", target_bir_lowering=False, num_devices=1)
    dram = {k: nc.dram_tensor("in_" + k, v.shape, mybir.dt.from_np(v.dtype), kind="ExternalInput").ap() for k, v in arrays.items()}
    out = nc.dram_tensor("out_t", (D, T), F32, kind="ExternalOutput").ap()
    build_trunk(nc, dram, out)
    result = run_bass_kernel_spmd(nc, [{"in_" + k: v for k, v in arrays.items()}], core_ids=[0])
    return result.results[0]["out_t"].T[None]
```
